# Optimizing a Trainium2 kernel written in Bass

```python
import math
import jax, jax.numpy as jnp
from jax import lax
import numpy as np

D_MODEL = 2048
BATCH = 1
SEQ = 256
DEPTH = 1

CHUNK = 64
MEM_TOKENS = 256
NORM_EPS = 1e-6

GDN_HEAD_DIM = 128
GDN_WIDTH = D_MODEL // 2
GDN_HEADS = GDN_WIDTH // GDN_HEAD_DIM
GDN_CONV = 4
GDN_COLS = 4 * GDN_WIDTH + 2 * GDN_HEADS

RWKV_HEAD_DIM = 64
RWKV_WIDTH = D_MODEL - GDN_WIDTH
RWKV_HEADS = RWKV_WIDTH // RWKV_HEAD_DIM
RWKV_DECAY_RANK = 64
RWKV_AAA_RANK = 64
RWKV_GATE_RANK = 160
RWKV_GN_EPS = 64e-5
RWKV_COLS = 3 * RWKV_WIDTH + RWKV_DECAY_RANK + RWKV_AAA_RANK + RWKV_GATE_RANK

IN_PROJ_COLS = GDN_COLS + RWKV_COLS

XA_HEADS = 4
XA_HEAD_DIM = D_MODEL // XA_HEADS

D_FF = 4 * D_MODEL


def _rmsnorm(x, gain, eps=NORM_EPS):
    xf = x.astype(jnp.float32)
    y = xf * lax.rsqrt(jnp.mean(xf * xf, axis=-1, keepdims=True) + eps)
    return (y * gain.astype(jnp.float32)).astype(x.dtype)

def _l2norm(x, eps=1e-6):
    return x * lax.rsqrt(jnp.sum(x * x, axis=-1, keepdims=True) + eps)

def _causal_depthwise_conv(x, w):
    K, C = w.shape
    return lax.conv_general_dilated(
        x, w[:, None, :].astype(x.dtype), window_strides=(1,),
        padding=((K - 1, 0),), dimension_numbers=("NWC", "WIO", "NWC"),
        feature_group_count=C)

def _token_shift(y):
    return jnp.pad(y, ((0, 0), (1, 0), (0, 0)))[:, :-1]

def _gated_delta_chunked(q, k, v, g, beta):
    B, T, H, Dk = q.shape
    Dv = v.shape[-1]
    NC = T // CHUNK

    def chunks4(t):
        return t.reshape(B, NC, CHUNK, H, t.shape[-1]).transpose(0, 3, 1, 2, 4)

    def chunks3(t):
        return t.reshape(B, NC, CHUNK, H).transpose(0, 3, 1, 2)

    qc, kc, vc = chunks4(q), chunks4(k), chunks4(v)
    bc = chunks3(beta)
    G = jnp.cumsum(chunks3(g), axis=-1)
    idx = jnp.arange(CHUNK)
    causal = idx[:, None] >= idx[None, :]
    strict = idx[:, None] > idx[None, :]
    diff = G[..., :, None] - G[..., None, :]
    gamma = jnp.where(causal, jnp.exp(jnp.where(causal, diff, 0.0)), 0.0)

    kb = kc * bc[..., None]
    vb = vc * bc[..., None]
    M = jnp.where(strict, jnp.einsum("bhnid,bhnjd->bhnij", kb, kc) * gamma, 0.0)
    eye = jnp.eye(CHUNK, dtype=q.dtype)
    rhs = jnp.concatenate([vb, kb * jnp.exp(G)[..., None]], axis=-1)
    sol = lax.linalg.triangular_solve(M + eye, rhs, left_side=True, lower=True,
                                      unit_diagonal=True)
    U, W = sol[..., :Dv], sol[..., Dv:]
    Aqk = jnp.einsum("bhnid,bhnjd->bhnij", qc, kc) * gamma
    q_dec = qc * jnp.exp(G)[..., None]
    G_last = G[..., -1]
    k_tail = kc * jnp.exp(G_last[..., None] - G)[..., None]

    def step(S, xs):
        U_c, W_c, qd, kt, A_c, gl = xs
        v_new = U_c - jnp.einsum("bhik,bhkv->bhiv", W_c, S)
        o = jnp.einsum("bhik,bhkv->bhiv", qd, S) + jnp.einsum("bhij,bhjv->bhiv", A_c, v_new)
        S = S * jnp.exp(gl)[..., None, None] + jnp.einsum("bhik,bhiv->bhkv", kt, v_new)
        return S, o

    xs = tuple(jnp.moveaxis(t, 2, 0) for t in (U, W, q_dec, k_tail, Aqk, G_last))
    S0 = jnp.zeros((B, H, Dk, Dv), q.dtype)
    _, o = lax.scan(step, S0, xs)
    return o.transpose(1, 0, 3, 2, 4).reshape(B, T, H, Dv)

def _gdn_group(y_g, conv_w, A_log, dt_bias, norm_w):
    B, T, _ = y_g.shape
    H, Dh, GW = GDN_HEADS, GDN_HEAD_DIM, GDN_WIDTH
    qkv = jax.nn.silu(_causal_depthwise_conv(y_g[..., :3 * GW], conv_w)).astype(jnp.float32)
    q, k, v = [t.reshape(B, T, H, Dh) for t in jnp.split(qkv, 3, axis=-1)]
    q = _l2norm(q) * (Dh ** -0.5)
    k = _l2norm(k)
    yf = y_g.astype(jnp.float32)
    z = yf[..., 3 * GW:4 * GW].reshape(B, T, H, Dh)
    a_dt = yf[..., 4 * GW:4 * GW + H]
    b = yf[..., 4 * GW + H:4 * GW + 2 * H]
    g = -jnp.exp(A_log.astype(jnp.float32)) * jax.nn.softplus(a_dt + dt_bias.astype(jnp.float32))
    beta = jax.nn.sigmoid(b)
    o = _gated_delta_chunked(q, k, v, g, beta)
    o = o * lax.rsqrt(jnp.mean(o * o, axis=-1, keepdims=True) + NORM_EPS)
    o = o * norm_w.astype(jnp.float32) * jax.nn.silu(z)
    return o.reshape(B, T, GW)

def _rwkv7_scan(r, w, k, v, a_vec, b_vec):
    B, T, H, N = r.shape

    def step(S, xs):
        r_t, w_t, k_t, v_t, a_t, b_t = xs
        Sa = jnp.einsum("bhvk,bhk->bhv", S, a_t)
        S = S * w_t[:, :, None, :] + Sa[..., :, None] * b_t[..., None, :] \
            + v_t[..., :, None] * k_t[..., None, :]
        return S, jnp.einsum("bhvk,bhk->bhv", S, r_t)

    xs = tuple(jnp.moveaxis(t, 1, 0) for t in (r, w, k, v, a_vec, b_vec))
    S0 = jnp.zeros((B, H, N, N), r.dtype)
    _, o = lax.scan(step, S0, xs)
    return jnp.moveaxis(o, 0, 1)

def _rwkv_group(y_r, mu, w0, w2, a0, a2, g2, k_k, k_a, r_k, ln_w, ln_b):
    B, T, _ = y_r.shape
    H, N, W = RWKV_HEADS, RWKV_HEAD_DIM, RWKV_WIDTH
    y = y_r.astype(jnp.float32)
    y = y + (_token_shift(y) - y) * mu.astype(jnp.float32)
    r, k, v = y[..., :W], y[..., W:2 * W], y[..., 2 * W:3 * W]
    o0 = 3 * W
    w_lo = y[..., o0:o0 + RWKV_DECAY_RANK]
    a_lo = y[..., o0 + RWKV_DECAY_RANK:o0 + RWKV_DECAY_RANK + RWKV_AAA_RANK]
    g_lo = y[..., o0 + RWKV_DECAY_RANK + RWKV_AAA_RANK:]
    w_log = -jax.nn.softplus(-(w0 + jnp.tanh(w_lo) @ w2)) - 0.5
    decay = jnp.exp(-jnp.exp(w_log))
    a = jax.nn.sigmoid(a0 + a_lo @ a2)
    g = jax.nn.sigmoid(g_lo) @ g2

    def heads(t):
        return t.reshape(B, T, H, N)

    kk = _l2norm(heads(k * k_k))
    k = k * (1.0 + (a - 1.0) * k_a)
    r_h, k_h, v_h, a_h = heads(r), heads(k), heads(v), heads(a)
    o = _rwkv7_scan(r_h, heads(decay), k_h, v_h, -kk, kk * a_h)
    mean = jnp.mean(o, axis=-1, keepdims=True)
    var = jnp.mean(jnp.square(o - mean), axis=-1, keepdims=True)
    o = ((o - mean) * lax.rsqrt(var + RWKV_GN_EPS)).reshape(B, T, W) * ln_w + ln_b
    bonus = jnp.sum(r_h * k_h * r_k, axis=-1, keepdims=True) * v_h
    return (o + bonus.reshape(B, T, W)) * g

def _cross_attention(hn, mn, wq, wk, wv, wo):
    B, T, D = hn.shape
    M = mn.shape[1]
    q = (hn @ wq).reshape(B, T, XA_HEADS, XA_HEAD_DIM)
    k = (mn @ wk).reshape(B, M, XA_HEADS, XA_HEAD_DIM)
    v = (mn @ wv).reshape(B, M, XA_HEADS, XA_HEAD_DIM)
    s = jnp.einsum("bthd,bmhd->bhtm", q, k).astype(jnp.float32) * (XA_HEAD_DIM ** -0.5)
    p = jax.nn.softmax(s, axis=-1).astype(hn.dtype)
    o = jnp.einsum("bhtm,bmhd->bthd", p, v).reshape(B, T, D)
    return o @ wo

def first_inputs(seed: int = 0) -> dict:
    key = jax.random.key(seed)
    keys = jax.random.split(key, 32)
    counter = [0]

    def nk():
        counter[0] += 1
        return keys[counter[0] - 1]

    f32 = jnp.float32
    L, D = DEPTH, D_MODEL

    def nrm(shape, scale):
        return jax.random.normal(nk(), shape, f32) * scale

    def gain(shape):
        return 1.0 + nrm(shape, 0.02)

    x = nrm((BATCH, SEQ, D), 1.0)
    mem = nrm((BATCH, MEM_TOKENS, D), 1.0)
    norm_mix = gain((L, D))
    w_in = nrm((L, D, IN_PROJ_COLS), D ** -0.5)
    gdn_conv_w = nrm((L, GDN_CONV, 3 * GDN_WIDTH), GDN_CONV ** -0.5)
    gdn_A_log = jnp.log(jax.random.uniform(nk(), (L, GDN_HEADS), f32, 1.0, 16.0))
    dt = jnp.exp(jax.random.uniform(nk(), (L, GDN_HEADS), f32, math.log(1e-3), math.log(1e-1)))
    gdn_dt_bias = dt + jnp.log(-jnp.expm1(-dt))
    gdn_norm_w = gain((L, GDN_HEAD_DIM))
    rwkv_mu = jax.random.uniform(nk(), (L, RWKV_COLS), f32, 0.0, 1.0)
    rwkv_w0 = jax.random.uniform(nk(), (L, RWKV_WIDTH), f32, -6.0, -0.5)
    rwkv_w2 = nrm((L, RWKV_DECAY_RANK, RWKV_WIDTH), 0.2 * RWKV_DECAY_RANK ** -0.5)
    rwkv_a0 = nrm((L, RWKV_WIDTH), 0.1)
    rwkv_a2 = nrm((L, RWKV_AAA_RANK, RWKV_WIDTH), 0.5 * RWKV_AAA_RANK ** -0.5)
    rwkv_g2 = nrm((L, RWKV_GATE_RANK, RWKV_WIDTH), RWKV_GATE_RANK ** -0.5)
    rwkv_k_k = 0.85 + nrm((L, RWKV_WIDTH), 0.02)
    rwkv_k_a = gain((L, RWKV_WIDTH))
    rwkv_r_k = nrm((L, RWKV_HEADS, RWKV_HEAD_DIM), 0.1)
    rwkv_ln_w = gain((L, RWKV_WIDTH))
    rwkv_ln_b = nrm((L, RWKV_WIDTH), 0.01)
    w_out = nrm((L, D, D), D ** -0.5)
    norm_xattn = gain((L, D))
    norm_mem = gain((L, D))
    xattn_wq = nrm((L, D, D), D ** -0.5)
    xattn_wk = nrm((L, D, D), D ** -0.5)
    xattn_wv = nrm((L, D, D), D ** -0.5)
    xattn_wo = nrm((L, D, D), D ** -0.5)
    norm_mlp = gain((L, D))
    mlp_w_up = nrm((L, D, D_FF), D ** -0.5)
    mlp_w_down = nrm((L, D_FF, D), D_FF ** -0.5)
    norm_final = gain((D,))
    return {"x": x, "mem": mem, "norm_mix": norm_mix, "w_in": w_in,
            "gdn_conv_w": gdn_conv_w, "gdn_A_log": gdn_A_log, "gdn_dt_bias": gdn_dt_bias,
            "gdn_norm_w": gdn_norm_w, "rwkv_mu": rwkv_mu, "rwkv_w0": rwkv_w0,
            "rwkv_w2": rwkv_w2, "rwkv_a0": rwkv_a0, "rwkv_a2": rwkv_a2, "rwkv_g2": rwkv_g2,
            "rwkv_k_k": rwkv_k_k, "rwkv_k_a": rwkv_k_a, "rwkv_r_k": rwkv_r_k,
            "rwkv_ln_w": rwkv_ln_w, "rwkv_ln_b": rwkv_ln_b, "w_out": w_out,
            "norm_xattn": norm_xattn, "norm_mem": norm_mem, "xattn_wq": xattn_wq,
            "xattn_wk": xattn_wk, "xattn_wv": xattn_wv, "xattn_wo": xattn_wo,
            "norm_mlp": norm_mlp, "mlp_w_up": mlp_w_up, "mlp_w_down": mlp_w_down,
            "norm_final": norm_final}

def first_block(x, mem, norm_mix, w_in, gdn_conv_w, gdn_A_log, gdn_dt_bias, gdn_norm_w,
              rwkv_mu, rwkv_w0, rwkv_w2, rwkv_a0, rwkv_a2, rwkv_g2, rwkv_k_k, rwkv_k_a,
              rwkv_r_k, rwkv_ln_w, rwkv_ln_b, w_out, norm_xattn, norm_mem, xattn_wq,
              xattn_wk, xattn_wv, xattn_wo, norm_mlp, mlp_w_up, mlp_w_down, norm_final):
    h = x
    for l in range(DEPTH):
        xn = _rmsnorm(h, norm_mix[l])
        y = xn @ w_in[l]
        o_gdn = _gdn_group(y[..., :GDN_COLS], gdn_conv_w[l], gdn_A_log[l],
                           gdn_dt_bias[l], gdn_norm_w[l])
        o_rwkv = _rwkv_group(y[..., GDN_COLS:], rwkv_mu[l], rwkv_w0[l], rwkv_w2[l],
                             rwkv_a0[l], rwkv_a2[l], rwkv_g2[l], rwkv_k_k[l], rwkv_k_a[l],
                             rwkv_r_k[l], rwkv_ln_w[l], rwkv_ln_b[l])
        mixed = jnp.concatenate([o_gdn, o_rwkv], axis=-1).astype(h.dtype)
        h = h + mixed @ w_out[l]
        h = h + _cross_attention(_rmsnorm(h, norm_xattn[l]), _rmsnorm(mem, norm_mem[l]),
                                 xattn_wq[l], xattn_wk[l], xattn_wv[l], xattn_wo[l])
        hn = _rmsnorm(h, norm_mlp[l])
        h = h + jnp.square(jax.nn.relu(hn @ mlp_w_up[l])) @ mlp_w_down[l]
    return _rmsnorm(h, norm_final)


HEAD_DIM = 64
MIX_WIDTH = D_MODEL
N_HEADS_A = (MIX_WIDTH // 2) // HEAD_DIM
N_HEADS_B = (MIX_WIDTH // 2) // HEAD_DIM
WIDTH_A = N_HEADS_A * HEAD_DIM
WIDTH_B = N_HEADS_B * HEAD_DIM
IN_WIDTH = 4 * WIDTH_A + 4 * WIDTH_B
DILATED_CONFIGS = ((128, 1), (512, 4), (2048, 16))
NUM_BUCKETS = 32
T5_MAX_DISTANCE = 1024
GRID_W = 64
NA_ROWS = 8
NA_COLS = 16
NA_COL_BLOCKS = GRID_W // NA_COLS
NA_KEY_COLS = 2 * NA_COLS
DEEPNORM_ALPHA = (2.0 * DEPTH) ** 0.25
DEEPNORM_BETA = (8.0 * DEPTH) ** -0.25
LN_EPS = 1e-5
NEG_INF = -1e30


def _t5_buckets(rel):
    half = NUM_BUCKETS // 2
    max_exact = half // 2
    n = np.abs(rel)
    large = max_exact + (np.log(np.maximum(n, 1) / max_exact)
                         / np.log(T5_MAX_DISTANCE / max_exact)
                         * (half - max_exact)).astype(np.int64)
    large = np.minimum(large, half - 1)
    return ((rel > 0).astype(np.int64) * half + np.where(n < max_exact, n, large)).astype(np.int32)

def _layer_norm(x, g, b):
    xf = x.astype(jnp.float32)
    mu = xf.mean(-1, keepdims=True)
    var = jnp.square(xf - mu).mean(-1, keepdims=True)
    return ((xf - mu) * lax.rsqrt(var + LN_EPS) * g.astype(jnp.float32)
            + b.astype(jnp.float32)).astype(x.dtype)

def _dilated_branch(q, k, v, t5_table, window, dilation):
    B, H, S, hd = q.shape
    blk = window // (2 * dilation)
    L = S // dilation
    nb = -(-L // blk)
    Lp = nb * blk
    scale = HEAD_DIM ** -0.5

    def strided(a):
        return a.reshape(B, H, L, dilation, hd).transpose(0, 1, 3, 2, 4)

    qs = jnp.pad(strided(q), ((0, 0), (0, 0), (0, 0), (0, Lp - L), (0, 0)))
    qs = qs.reshape(B, H, dilation, nb, blk, hd)

    def key_blocks(a):
        a = jnp.pad(strided(a), ((0, 0), (0, 0), (0, 0), (blk, Lp - L + blk), (0, 0)))
        a = a.reshape(B, H, dilation, nb + 2, blk, hd)
        return jnp.concatenate([a[:, :, :, :nb], a[:, :, :, 1:nb + 1], a[:, :, :, 2:]], axis=4)

    ks, vs = key_blocks(k), key_blocks(v)
    rel = np.arange(3 * blk)[None, :] - blk - np.arange(blk)[:, None]
    band = np.abs(rel) <= blk
    key_abs = (np.arange(nb)[:, None] - 1) * blk + np.arange(3 * blk)[None, :]
    valid = (key_abs >= 0) & (key_abs < L)
    mask = band[None] & valid[:, None, :]
    bias = jnp.take(t5_table, _t5_buckets(rel * dilation), axis=0)
    bias = jnp.moveaxis(bias.astype(jnp.float32), -1, 0)

    s = jnp.einsum('bhrnqd,bhrnkd->bhrnqk', qs, ks).astype(jnp.float32) * scale
    s = jnp.where(mask, s + bias[None, :, None, None], NEG_INF)
    m = s.max(-1, keepdims=True)
    p = jnp.exp(s - m)
    den = p.sum(-1, keepdims=True)
    o = jnp.einsum('bhrnqk,bhrnkd->bhrnqd', p, vs.astype(jnp.float32)) / den
    lse = (m + jnp.log(den))[..., 0]
    o = o.reshape(B, H, dilation, Lp, hd)[:, :, :, :L].transpose(0, 1, 3, 2, 4).reshape(B, H, S, hd)
    lse = lse.reshape(B, H, dilation, Lp)[..., :L].transpose(0, 1, 3, 2).reshape(B, H, S)
    return o, lse

def _dilated_attention(q, k, v, t5_table):
    outs, lses = [], []
    for window, dilation in DILATED_CONFIGS:
        o, lse = _dilated_branch(q, k, v, t5_table, window, dilation)
        outs.append(o)
        lses.append(lse)
    wts = jax.nn.softmax(jnp.stack(lses, 0), axis=0)
    return jnp.einsum('cbhs,cbhsd->bhsd', wts, jnp.stack(outs, 0))

def _neighbourhood_attention(q, k, v, rpb):
    B, H, S, hd = q.shape
    rows = S // GRID_W
    kr = min(NA_ROWS, rows)
    scale = HEAD_DIM ** -0.5
    row_start = np.clip(np.arange(rows) - kr // 2, 0, rows - kr)
    row_idx = row_start[:, None] + np.arange(kr)
    qcol = np.arange(GRID_W).reshape(NA_COL_BLOCKS, NA_COLS)
    blk_start = np.clip(qcol[:, 0] - NA_COLS // 2, 0, GRID_W - NA_KEY_COLS)
    col_idx = blk_start[:, None] + np.arange(NA_KEY_COLS)
    q_start = np.clip(qcol - NA_COLS // 2, 0, GRID_W - NA_COLS)
    kcol = col_idx[:, None, :]
    col_mask = (kcol >= q_start[:, :, None]) & (kcol < q_start[:, :, None] + NA_COLS)
    dcol = np.clip(kcol - qcol[:, :, None], -(NA_COLS - 1), NA_COLS - 1)
    drow = row_idx - np.arange(rows)[:, None]
    ri = (drow + NA_ROWS - 1)[None, :, None, :, None]
    ci = (dcol + NA_COLS - 1)[:, None, :, None, :]
    bias = rpb.astype(jnp.float32)[:, ri, ci]
    bias = jnp.where(col_mask[:, None, :, None, :], bias, NEG_INF)
    bias = bias.transpose(1, 0, 2, 3, 4, 5).reshape(NA_COL_BLOCKS, H, rows, NA_COLS, kr * NA_KEY_COLS)

    qb = q.reshape(B, H, rows, NA_COL_BLOCKS, NA_COLS, hd).transpose(3, 0, 1, 2, 4, 5)
    kg = k.reshape(B, H, rows, GRID_W, hd)
    vg = v.reshape(B, H, rows, GRID_W, hd)

    def row_block(args):
        q_blk, cidx, bias_blk = args
        k_blk = jnp.take(kg, cidx, axis=3)[:, :, row_idx].reshape(B, H, rows, kr * NA_KEY_COLS, hd)
        v_blk = jnp.take(vg, cidx, axis=3)[:, :, row_idx].reshape(B, H, rows, kr * NA_KEY_COLS, hd)
        s = jnp.einsum('bhrqd,bhrkd->bhrqk', q_blk, k_blk).astype(jnp.float32) * scale + bias_blk[None]
        p = jax.nn.softmax(s, axis=-1)
        return jnp.einsum('bhrqk,bhrkd->bhrqd', p, v_blk.astype(jnp.float32))

    o = lax.map(row_block, (qb, jnp.asarray(col_idx, jnp.int32), bias))
    return o.transpose(1, 2, 3, 0, 4, 5).reshape(B, H, S, hd)

def second_inputs(seed: int = 0) -> dict:
    key = jax.random.key(seed)
    ks = jax.random.split(key, 7)
    x = jax.random.normal(ks[0], (BATCH, SEQ, D_MODEL), jnp.float32)
    col_scale = np.ones((IN_WIDTH,), np.float32)
    col_scale[2 * WIDTH_A:3 * WIDTH_A] = DEEPNORM_BETA
    col_scale[4 * WIDTH_A + 2 * WIDTH_B:4 * WIDTH_A + 3 * WIDTH_B] = DEEPNORM_BETA
    w_in = (jax.random.normal(ks[1], (DEPTH, D_MODEL, IN_WIDTH), jnp.float32)
            * D_MODEL ** -0.5 * jnp.asarray(col_scale))
    w_out = jax.random.normal(ks[2], (DEPTH, MIX_WIDTH, D_MODEL), jnp.float32) * (MIX_WIDTH ** -0.5 * DEEPNORM_BETA)
    t5_bias = jax.random.normal(ks[3], (NUM_BUCKETS, N_HEADS_A), jnp.float32) * 0.5
    na_rpb = jax.random.normal(ks[4], (DEPTH, N_HEADS_B, 2 * NA_ROWS - 1, 2 * NA_COLS - 1), jnp.float32) * 0.5
    ln_gain = 1.0 + 0.05 * jax.random.normal(ks[5], (DEPTH, D_MODEL), jnp.float32)
    ln_bias = 0.02 * jax.random.normal(ks[6], (DEPTH, D_MODEL), jnp.float32)
    return {"x": x, "w_in": w_in, "w_out": w_out, "t5_bias": t5_bias,
            "na_rpb": na_rpb, "ln_gain": ln_gain, "ln_bias": ln_bias}

def second_block(x, w_in, w_out, t5_bias, na_rpb, ln_gain, ln_bias):
    B, S, _ = x.shape
    splits = np.cumsum([WIDTH_A] * 4 + [WIDTH_B] * 3)

    def heads(a, n):
        return a.reshape(B, S, n, HEAD_DIM).transpose(0, 2, 1, 3)

    def merge(o):
        return o.transpose(0, 2, 1, 3).reshape(B, S, -1)

    for layer in range(DEPTH):
        h = jnp.einsum('bsd,de->bse', x, w_in[layer])
        qa, ka, va, ga, qb, kb, vb, gb = jnp.split(h, splits, axis=-1)
        ya = _dilated_attention(heads(qa, N_HEADS_A), heads(ka, N_HEADS_A), heads(va, N_HEADS_A), t5_bias)
        yb = _neighbourhood_attention(heads(qb, N_HEADS_B), heads(kb, N_HEADS_B), heads(vb, N_HEADS_B), na_rpb[layer])
        ya = merge(ya) * jax.nn.silu(ga.astype(jnp.float32))
        yb = merge(yb) * jax.nn.silu(gb.astype(jnp.float32))
        y = jnp.concatenate([ya, yb], axis=-1).astype(x.dtype)
        out = jnp.einsum('bse,ed->bsd', y, w_out[layer])
        x = _layer_norm(DEEPNORM_ALPHA * x + out, ln_gain[layer], ln_bias[layer])
    return x


def setup_inputs(seed=0):
    out = dict(first_inputs(seed))
    for name, value in second_inputs(seed + 1).items():
        if name != "x":
            out[name + "_2"] = value
    return out


def reference(
    x, mem, norm_mix, w_in, gdn_conv_w, gdn_A_log, gdn_dt_bias, gdn_norm_w, rwkv_mu, rwkv_w0,
    rwkv_w2, rwkv_a0, rwkv_a2, rwkv_g2, rwkv_k_k, rwkv_k_a, rwkv_r_k, rwkv_ln_w, rwkv_ln_b,
    w_out, norm_xattn, norm_mem, xattn_wq, xattn_wk, xattn_wv, xattn_wo, norm_mlp, mlp_w_up,
    mlp_w_down, norm_final, w_in_2, w_out_2, t5_bias_2, na_rpb_2, ln_gain_2, ln_bias_2,
):
    x = first_block(
        x, mem, norm_mix, w_in, gdn_conv_w, gdn_A_log, gdn_dt_bias, gdn_norm_w, rwkv_mu,
        rwkv_w0, rwkv_w2, rwkv_a0, rwkv_a2, rwkv_g2, rwkv_k_k, rwkv_k_a, rwkv_r_k, rwkv_ln_w,
        rwkv_ln_b, w_out, norm_xattn, norm_mem, xattn_wq, xattn_wk, xattn_wv, xattn_wo,
        norm_mlp, mlp_w_up, mlp_w_down, norm_final,
    )
    return second_block(
        x, w_in_2, w_out_2, t5_bias_2, na_rpb_2, ln_gain_2, ln_bias_2,
    )


_drawn_inputs = setup_inputs


def setup_inputs(seed=0):
    import zlib

    import numpy as np

    out = dict(_drawn_inputs(seed))
    spreads = {}
    factors = {'norm_mix': 2.908,
     'gdn_norm_w': 7.2,
     'rwkv_w2': 8.0,
     'rwkv_a0': 3.337,
     'rwkv_k_k': 24.762,
     'rwkv_k_a': 7.113,
     'rwkv_ln_w': 8.0,
     'rwkv_ln_b': 29.225,
     'norm_xattn': 8.0,
     'norm_mem': 8.0,
     'norm_mlp': 3.443,
     'norm_final': 2.847,
     't5_bias_2': 7.823,
     'na_rpb_2': 5.115,
     'ln_bias_2': 2.842}
    for name, (base, spread) in spreads.items():
        noise = np.random.default_rng([zlib.crc32(name.encode()), seed]).standard_normal(out[name].shape)
        drawn = base * np.exp(spread * noise) if base else spread * noise
        out[name] = __import__('jax').numpy.asarray(drawn.astype(out[name].dtype))
    for name, factor in factors.items():
        out[name] = (out[name] * factor).astype(out[name].dtype)
    return out
```

```python
import math
from contextlib import ExitStack, contextmanager

import numpy as np

import concourse.bass as bass
from concourse import mybir

F32 = mybir.dt.float32
F32R = mybir.dt.float32r
BF16 = mybir.dt.bfloat16
ALU = mybir.AluOpType
ACT = mybir.ActivationFunctionType
AX = mybir.AxisListType
ds = bass.ds

P = 128
D = 2048
T = 256
NT = T // P
KT = D // P
SLOT_K = 4
COLS = 512
SLOTS = KT // SLOT_K
NORM_EPS = 1e-6

GDN_H, GDN_D = 8, 128
GDN_W = GDN_H * GDN_D
GDN_COLS = 4 * GDN_W + 2 * GDN_H
RW_H, RW_D, RW_C = 16, 64, 64
RW_W = RW_H * RW_D
RW_PAIRS = RW_H // 2
LORA_W, LORA_A, LORA_G = 64, 64, 160
LORA = LORA_W + LORA_A + LORA_G
LORA_COL = GDN_COLS + 3 * RW_W
RW_EPS = 64e-5
XH, XD = 4, 512
AH, AD = 16, 64
D_FF = 4 * D
LN_EPS = 1e-5
ALPHA = 2.0 ** 0.25
GRID, NA_ROW = 64, 7 * P
NEG = -8e30


def _columns():
    at, out = 0, {}
    for name, n in (("ident", P), ("ones", 2 * P), ("blockones", P), ("le", P), ("gt", P), ("gdn_mask", 2 * P),
                    ("level", 7 * P), ("rw_mask", 4 * P), ("headsel", 2), ("reset", T), ("na_mask", 64)):
        out[name] = (at, n)
        at += n
    return out, at


CONST, N_CONST = _columns()


def _bucket(rel):
    half, exact = 16, 8
    n = np.abs(rel)
    large = exact + (np.log(np.maximum(n, 1) / exact) / np.log(1024 / exact) * (half - exact)).astype(np.int64)
    return (rel > 0) * half + np.where(n < exact, n, np.minimum(large, half - 1))


def constants():
    c = np.zeros((P, N_CONST), np.float32)
    j, i = np.arange(P)[:, None], np.arange(P)[None, :]

    def put(name, a):
        at, n = CONST[name]
        c[:, at:at + n] = a.reshape(P, n)

    put("ident", (i == j) * 1.0)
    put("ones", np.ones((P, 2 * P)))
    put("blockones", (i // RW_D == j // RW_D) * 1.0)
    put("le", (j <= i) * 1.0)
    put("gt", (j > i) * 1.0)
    put("gdn_mask", np.stack([j < i, j <= i], 1) * 1.0)
    put("level", np.stack([((i >> l + 1) == (j >> l + 1)) & ((i >> l) % 2 == 1) & ((j >> l) % 2 == 0)
                           for l in range(7)], 1) * 1.0)
    same = i // RW_C == j // RW_C
    put("rw_mask", np.stack([same & (j < i), same & (j <= i)] * 2, 1) * 1.0)
    put("headsel", (j // RW_D == np.arange(2)[None, :]) * 1.0)
    put("reset", np.broadcast_to(np.arange(T) % RW_C != 0, (P, T)) * 1.0)
    q, k = np.arange(P)[:, None] % 64, np.arange(64)[None, :]
    start = np.clip(q - 8, 0, 48)
    put("na_mask", np.where((k >= start) & (k < start + 16), 0.0, NEG))
    rel = np.arange(512) - 255
    onehot = (_bucket(rel)[None, :] == np.arange(32)[:, None]) * 1.0
    count = (np.abs(rel) <= 64) * 1.0 + (rel % 4 == 0) + (rel % 16 == 0)
    logs = np.where(count > 0, 8.0 * np.log(np.maximum(count, 1)), NEG)
    dil = np.concatenate([onehot, np.broadcast_to(logs, (32, 512))], 1).astype(np.float32)
    return {"consts": c, "dilated": dil}


class Lin:

    def __init__(self, c=0, steps=()):
        self.c, self.steps = c, tuple(steps)

    def __add__(self, n):
        return Lin(self.c + n, self.steps)

    def stepped(self, loop, step):
        return Lin(self.c, self.steps + ((loop, step),))

    def times(self, k):
        return Lin(self.c * k, [(l, s * k) for l, s in self.steps])

    def value(self):
        v, live = self.c, []
        for loop, step in self.steps:
            if loop.closed:
                v += step * (loop.n - 1)
            elif step:
                live.append(loop.i * step)
        for x in live:
            v = x + v
        return v


class Loop:
    def __init__(self, i, n):
        self.i, self.n, self.closed = i, n, False


class Counter:
    def __init__(self, name, sem=None):
        self.name, self.sem, self.at = name, sem, Lin()

    def now(self):
        return self.sem, self.at


class Lane(Counter):

    def __init__(self, nc, ctx, name, engine):
        super().__init__(name, ctx.enter_context(nc.semaphore("done_" + name)))
        self.engine, self.ordered = engine, name in ("scalar", "vector", "gpsimd")

    def done(self, ins):
        ins.then_inc(self.sem, 1)
        self.at = self.at + 1
        return self.sem, self.at


def on(lane, *tokens):
    wait(lane, *tokens, lane.now() if lane.ordered else None)
    return lane.engine


def wait(lane, *tokens):
    latest = {}
    for t in tokens:
        if t is not None:
            key = id(t[0]), t[1].steps
            if key not in latest or latest[key][1].c < t[1].c:
                latest[key] = t
    for sem, at in latest.values():
        if at.c > 0 or at.steps:
            lane.engine.wait_ge(sem, at.value())


class Program:
    def __init__(self, nc, ctx, plan):
        self.nc, self.ctx, self.plan = nc, ctx, plan
        self.pe = Lane(nc, ctx, "tensor", nc.tensor)
        self.act = Lane(nc, ctx, "scalar", nc.scalar)
        self.dve = Lane(nc, ctx, "vector", nc.vector)
        self.pool = Lane(nc, ctx, "gpsimd", nc.gpsimd)
        self.sp = Lane(nc, ctx, "sync", nc.sync)
        self.lanes = [self.pe, self.act, self.dve, self.pool]
        self.counters = list(self.lanes)
        self.n_names = 0

    def sb(self, name, shape, dt=F32, ctx=None):
        return (ctx or self.ctx).enter_context(self.nc.sbuf_tensor(name, shape, dt))

    def counter(self, name, sem=None):
        c = Counter(name, sem)
        self.counters.append(c)
        return c

    def sem(self, name):
        return self.ctx.enter_context(self.nc.semaphore(name))

    def dma_sem(self, name):
        return self.counter(name, self.sem(name))

    def dma(self, lane, counter, out, in_, **kw):
        lane.engine.dma_start(out, in_, **kw).then_inc(counter.sem, 16)
        counter.at = counter.at + 16
        return counter.sem, counter.at

    @contextmanager
    def loop(self, name, n):
        starts = [c.at for c in self.counters]
        with self.nc.Fori(0, n) as i:
            loop = Loop(i, n)
            for c, s in zip(self.counters, starts):
                c.at = s.stepped(loop, self.plan.get((name, c.name), 0))
            yield loop
        loop.closed = True
        for c, s in zip(self.counters, starts):
            gain = c.at.c - s.c
            self.plan[(name, c.name)] = gain
            c.at = s + n * gain

    def join(self, *lanes):
        marks = [x.now() for x in self.lanes]
        for lane in lanes or self.lanes:
            wait(lane, *[m for x, m in zip(self.lanes, marks) if x is not lane])


def bc(ap, *shape):
    return ap.to_broadcast(list(shape))


class Stream:

    def __init__(self, p):
        self.p, nc = p, p.nc
        self.raw = [p.sb(f"weights_raw{j}", [P, SLOT_K, COLS]) for j in range(SLOTS)]
        self.head = [p.sb(f"weights_head{j}", [P, SLOT_K, COLS], F32R) for j in range(2)]
        self.rest = [p.sb(f"weights_rest{j}", [P, SLOT_K, COLS], F32R) for j in range(2)]
        self.arrived = [p.sem(f"weights_arrived{j}") for j in range(SLOTS)]
        self.s_head, self.s_rest, self.s_used = (p.sem("weights_" + x) for x in ("head_made", "rest_made", "used"))
        self.evacuated = [p.sem(f"product_bank{g}_read") for g in range(2)]
        self.banks = [p.ps[0], p.ps[1]]
        self.block_no = p.counter("block")

    def used(self, block, j):
        return self.s_used, block.times(SLOTS) + (j + 1)

    def last_used(self):
        return self.used(self.block_no.at + (-1), SLOTS - 1)

    def load(self, block, j, parts):
        sp, n = self.p.sp, 0
        if block.c or block.steps:
            wait(sp, (self.s_rest, (block + (-1)).times(SLOTS) + (j + 1)))
        for ap in parts:
            w = ap.shape[1]
            sp.engine.dma_start(self.raw[j][:, :, n:n + w], ap.rearrange("(k p) n -> p k n", p=P)) \
                .then_inc(self.arrived[j], 16)
            n += w

    def split(self, block, j, cols=COLS):
        p = self.p
        raw, head, rest = self.raw[j], self.head[j % 2], self.rest[j % 2]
        wait(p.act, (self.arrived[j], block.times(16) + 32))
        if j >= 2:
            wait(p.act, self.used(block, j - 2))
        elif block.c or block.steps:
            wait(p.act, self.used(block + (-1), j + 2))
        p.act.engine.activation(head[:, :, 0:cols], raw[:, :, 0:cols], ACT.Copy).then_inc(self.s_head, 1)
        wait(p.dve, (self.s_head, block.times(SLOTS) + (j + 1)))
        p.dve.engine.tensor_tensor(rest[:, :, 0:cols], raw[:, :, 0:cols], head[:, :, 0:cols].bitcast(F32),
                                   ALU.subtract).then_inc(self.s_rest, 1)

    def block(self, source, operand, transposed, read, cols=COLS, last=False, ready=(), after=None):
        p, pe = self.p, self.p.pe
        head_x, rest_x = operand
        block = self.block_no.at
        self.block_no.at = block + 1
        wait(pe, *ready)
        banks = range((cols + 2 * P - 1) // (2 * P)) if transposed else range(NT)
        for j in range(SLOTS):
            self.load(block, j, source(j))
            if j + 1 < SLOTS:
                self.split(block, j + 1, cols)
            elif not last:
                self.split(block + 1, 0)
            wait(pe, (self.s_rest, block.times(SLOTS) + (j + 1)))
            head, rest = self.head[j % 2], self.rest[j % 2]
            for g in banks:
                bank = self.banks[g]
                if j == 0 and (block.c or block.steps):
                    wait(pe, (self.evacuated[g], block))
                ends = range(2 * g, min(2 * g + 2, (cols + P - 1) // P)) if transposed else (g,)
                for c in ends:
                    for k in range(SLOT_K):
                        kt = j * SLOT_K + k
                        for a in range(3):
                            w = (head, rest, head)[a]
                            x = (head_x, head_x, rest_x)[a]
                            if transposed:
                                w = (head, head, rest)[a]
                                x = (head_x, rest_x, head_x)[a]
                            kw = {"start": kt == 0 and a == 0 and c == ends[0], "skip_group_check": True,
                                  "stop": kt == KT - 1 and a == 2}
                            if transposed:
                                o = (c - ends[0]) * T
                                m = pe.engine.matmul(bank[:, o:o + T], w[:, k, c * P:(c + 1) * P], x[:, kt, :], **kw)
                            else:
                                m = pe.engine.matmul(bank[:, :], x[:, kt, g * P:(g + 1) * P], w[:, k, :], **kw)
                        last_product = g == banks[-1] and c == ends[-1] and k == SLOT_K - 1
                        if last_product:
                            m.then_inc(self.s_used, 1)
                        elif j == SLOTS - 1 and c == ends[-1] and k == SLOT_K - 1:
                            first_done = pe.done(m)
                        if k % 2:
                            yield
                if j == SLOTS - 1:
                    done = self.used(block, j) if g == banks[-1] else first_done
                    read(g, done).then_inc(self.evacuated[g], 1)
            if after:
                if j == SLOTS - 1:
                    for g in banks:
                        after(g)

    def start(self, source, cols):
        self.split(Lin(), 0, cols)


def run(pieces):
    for _ in pieces:
        pass


class Filler:

    def __init__(self, pieces=None):
        self.pieces = pieces

    def __call__(self, n=1):
        for _ in range(n):
            if self.pieces is not None:
                next(self.pieces, None)

    def finish(self):
        if self.pieces is not None:
            run(self.pieces)


def columns(w, first, rows=0):
    return lambda j: [w[ds(rows + j * SLOT_K * P, SLOT_K * P), ds(first, COLS)]]


def weave(pieces, steps, n, first=2):
    steps = list(steps)
    room = max(n - first - 1, 1)
    given = 0
    for k, _ in enumerate(pieces):
        while given < len(steps) and k >= first + given * room // len(steps):
            steps[given]()
            given += 1
    for step in steps[given:]:
        step()


def norm_scale(p, lane_tokens, x, eps, ctx):
    pe, act, dve, pool = p.lanes
    ss = p.ss
    for t in range(NT):
        sq = act.done(on(act, *lane_tokens).activation(p.junk[:, :], x[:, t, :], ACT.Square,
                                                       accum_out=ss[:, t:t + 1]))
    mean = pool.done(on(pool, sq).tensor_scalar(ss[:, 2:4], ss[:, 0:2], 1.0 / D, eps, ALU.mult, ALU.add))
    return pool.done(on(pool, mean).tensor_tensor(p.rstd[:, 0:2], ss[:, 2:4], p.minus_half[:, 0:2], ALU.pow))


def to_operand(p, x, diag_of, gain, operand, after=(), free=()):
    pe, act, dve, pool = p.lanes
    head, rest = operand
    banks = p.ps[2:8]
    read = [None] * len(banks)
    for pair in range(KT // 2):
        n = pair % len(banks)
        bank = banks[n]
        for c in range(2):
            for t in range(NT):
                ct = 2 * pair + c
                m = on(pe, *(after if pair == 0 else ()), read[n] if c + t == 0 else None).matmul(
                    bank[:, c * T + t * P:c * T + (t + 1) * P], x[:, t, ct * P:(ct + 1) * P], diag_of(t),
                    start=True, stop=True)
        turned = pe.done(m)
        for c in range(2):
            ct, src = 2 * pair + c, bank[:, c * T:(c + 1) * T]
            scale = 1.0 if gain is None else gain(ct)
            a = act.done(on(act, turned, *(free if pair + c == 0 else ())).activation(
                head[:, ct, :], src, ACT.Copy, scale=scale))
        for c in range(2):
            ct, src = 2 * pair + c, bank[:, c * T:(c + 1) * T]
            out, h = rest[:, ct, :], head[:, ct, :].bitcast(F32)
            eng = on(dve, a, *(free if pair + c == 0 else ()))
            if gain is None:
                d = dve.done(eng.tensor_tensor(out, src, h, ALU.subtract))
            else:
                d = dve.done(eng.scalar_tensor_tensor(out=out, in0=src, scalar=gain(ct), in1=h, op0=ALU.mult,
                                                      op1=ALU.subtract))
        read[n] = d
    return d


def norm_to_operand(p, x, eps, gain, operand, after=(), free=()):
    pe, act, dve, pool = p.lanes
    scaled = norm_scale(p, after, x, eps, None)
    for t in range(NT):
        d = dve.done(on(dve, scaled, pe.now()).tensor_scalar(p.diag[:, t, :], p.c("ident"), p.rstd[:, t:t + 1],
                                                             None, ALU.mult))
    return to_operand(p, x, lambda t: p.diag[:, t, :], gain, operand, after=(d, *after), free=free)


PAR = {}
for _name, _n in (("norm_mix", 16), ("norm_xattn", 16), ("norm_mem", 16), ("norm_mlp", 16), ("rwkv_w0", 8),
                  ("rwkv_a0", 8), ("rwkv_k_k", 8), ("rwkv_k_a", 8), ("rwkv_r_k", 8), ("rwkv_ln_w", 8),
                  ("rwkv_ln_b", 8), ("gdn_norm_w", 1), ("mu_lora", 3)):
    PAR[_name] = sum(n for _, n in PAR.values()), _n
PAR["conv"] = 128, 96
PAR["mu"] = 224, 24


def build_program(nc, t, out, plan):
    with ExitStack() as ctx:
        p = Program(nc, ctx, plan)
        pe, act, dve, pool = p.lanes
        sp = p.sp
        p.ps = [ctx.enter_context(nc.psum_tensor(f"bank{i}", [P, 512], F32)) for i in range(8)]
        s = Stream(p)
        operand = p.sb("operand_head", [P, KT, T], F32R), p.sb("operand_rest", [P, KT, T], F32R)
        cst = p.sb("constants", [P, N_CONST])
        par = p.sb("parameters", [P, 2 * P])
        p.junk = p.sb("junk", [P, D], BF16)
        p.ss, p.rstd = p.sb("square_sums", [P, 4]), p.sb("rstd", [P, 4])
        p.minus_half = p.sb("minus_half", [P, 16])
        p.diag = p.sb("diagonals", [P, NT, P])
        a_dt = p.sb("a_log_dt_bias", [P, 2, GDN_H])
        p.c = lambda name: cst[:, CONST[name][0]:CONST[name][0] + CONST[name][1]]

        def pcol(name, k=0):
            at = PAR[name][0] + k
            return par[:, at:at + 1]

        t5_store = nc.dram_tensor("t5_store", (AH, P, 2 * T), F32, kind="Internal").ap()
        na_store = nc.dram_tensor("na_store", (AH, GRID, NA_ROW), F32, kind="Internal").ap()
        w = {n: t[n][0] for n in ("w_in", "w_out", "xattn_wq", "xattn_wk", "xattn_wv", "xattn_wo", "mlp_w_up",
                                  "mlp_w_down", "w_in_2", "w_out_2")}
        load_x, load_c, load_p = p.dma_sem("x_arrived"), p.dma_sem("constants_arrived"), p.dma_sem("rows_arrived")

        mix_ctx = ctx.enter_context(ExitStack())
        lora = p.sb("lora", [P, 3, T], ctx=mix_ctx)
        rbuf = p.sb("rwkv_rkv", [P, 24, T], ctx=mix_ctx)
        mixg = p.sb("gdn_out", [P, GDN_H, T], ctx=mix_ctx)
        gdn_ctx = mix_ctx.enter_context(ExitStack())
        ybuf = p.sb("gdn_qkvz", [P, 32, T], ctx=gdn_ctx)

        x_nat = ybuf[:, 16:32, :].rearrange("p a b -> p (a b)").rearrange("p (t d) -> p t d", t=NT)
        x_tok = t["x"][0].rearrange("(t p) d -> p t d", p=P)
        x_in = p.dma(sp, load_x, x_nat, x_tok)
        c_in = p.dma(sp, load_c, cst[:, :], t["consts"])
        rows = ybuf[:, 0, :].rearrange("p (a c) -> p a c", a=2)
        zeroed = pool.done(pool.engine.memset(rows, 0.0))
        halves = pool.done(pool.engine.memset(p.minus_half[:, :], -0.5))
        wait(sp, zeroed)
        for name, (at, n) in PAR.items():
            a, r = divmod(at, P)
            if name == "mu_lora":
                src = t["rwkv_mu"][0, 3 * RW_W:]
                p.dma(sp, load_p, rows[r:r + 2, a, :], src[0:256].rearrange("(n c) -> n c", c=P))
                p.dma(sp, load_p, rows[r + 2:r + 3, a, 0:32], src[256:288].rearrange("(n c) -> n c", n=1))
                continue
            if name == "conv":
                src = t["gdn_conv_w"][0].rearrange("k (n c) -> (k n) c", c=P)
            elif name == "mu":
                src = t["rwkv_mu"][0, 0:3 * RW_W].rearrange("(n c) -> n c", c=P)
            elif name == "rwkv_r_k":
                src = t[name][0].rearrange("(n a) c -> n (a c)", a=2)
            else:
                src = t[name][0].rearrange("(n c) -> n c", c=P)
            rows_in = p.dma(sp, load_p, rows[r:r + n, a, :], src)
        p.dma(sp, load_p, a_dt[:, 0, :], t["gdn_A_log"][0].partition_broadcast(P))
        rows_in = p.dma(sp, load_p, a_dt[:, 1, :], t["gdn_dt_bias"][0].partition_broadcast(P))

        for a in range(2):
            turned = pe.done(on(pe, rows_in, c_in).transpose(p.ps[2][:, a * P:(a + 1) * P], rows[:, a, :],
                                                             p.c("ident")))
        par_in = dve.done(on(dve, turned).tensor_copy(par[:, :], p.ps[2][:, 0:2 * P]))
        wait(dve, c_in)
        wait(pe, par_in)
        wait(act, par_in)
        wait(pool, halves)
        x_ready = norm_to_operand(p, x_nat, NORM_EPS, lambda ct: pcol("norm_mix", ct), operand, after=(x_in,))

        def narrow(j):
            r = slice(j * SLOT_K * P, (j + 1) * SLOT_K * P)
            return [w["w_in"][r, LORA_COL:LORA_COL + LORA], w["w_in"][r, 4 * GDN_W:4 * GDN_W + 96]]

        s.start(narrow, 3 * P)

        def read_lora(g, done):
            n = 2 if g == 0 else 1
            return on(act, done).activation(lora[:, 2 * g:2 * g + n, :].rearrange("p a b -> p (a b)"),
                                            s.banks[g][:, 0:n * T], ACT.Copy)

        run(s.block(narrow, operand, True, read_lora, cols=3 * P, ready=(x_ready,)))

        conv_ctx = gdn_ctx.enter_context(ExitStack())
        before = [p.sb(f"before_silu{g}", [P, 2, T], ctx=conv_ctx) for g in range(2)]
        filt = p.sb("filtered", [P, T], ctx=conv_ctx)
        half_tanh = p.sb("half_tanh", [P, T], ctx=conv_ctx)
        filt_w = p.sb("filter_taps", [P, 4, 4], ctx=conv_ctx)
        filt_rows = par[:, 128:224].rearrange("p (k c) -> p k c", k=4)

        def split_T(x, first, after, free):
            for k in range(0, x.shape[1], 4):
                to = slice(first + k, first + k + 4)
                a = act.done(on(act, *after, *free).activation(operand[0][:, to, :], x[:, k:k + 4, :], ACT.Copy))
                d = dve.done(on(dve, a).tensor_tensor(operand[1][:, to, :], x[:, k:k + 4, :],
                                                      operand[0][:, to, :].bitcast(F32), ALU.subtract))
            return d

        t5, dil = p.sb("t5_bias", [32, AH], ctx=conv_ctx), p.sb("dilated", [32, 4 * T], ctx=conv_ctx)
        t5_tab = p.sb("t5_table", [AH, 2 * T], ctx=conv_ctx)
        rpb, na_tab = p.sb("rpb", [AH, 7, 31], ctx=conv_ctx), p.sb("na_table", [AH, 7, P], ctx=conv_ctx)
        load_t, tab_stored = p.dma_sem("tables_arrived"), p.dma_sem("tables_stored")
        p.dma(act, load_t, t5[:, :], t["t5_bias_2"])
        p.dma(act, load_t, dil[:, :], t["dilated"])
        tab_in = p.dma(act, load_t, rpb[:, :, :], t["na_rpb_2"][0, :, 4:11, :])
        m = pe.done(on(pe, tab_in).matmul(p.ps[7][0:AH, :], t5[:, :], dil[:, 0:2 * T], start=True, stop=True))
        dve.done(on(dve, tab_in).memset(na_tab[:, :, :], 0.0))
        dve.done(on(dve).tensor_scalar(na_tab[:, :, 48:79], rpb[:, :, :], 8.0, None, ALU.mult))
        d = dve.done(on(dve, m).scalar_tensor_tensor(out=t5_tab[:, :], in0=p.ps[7][0:AH, :], scalar=8.0,
                                                     in1=dil[0:AH, 2 * T:4 * T], op0=ALU.mult, op1=ALU.add))
        wait(act, d)
        p.dma(act, tab_stored, t5_store, bc(t5_tab[:, :].unsqueeze(1), AH, P, 2 * T))
        p.dma(act, tab_stored, na_store, bc(na_tab[:, :, :].rearrange("h r j -> h (r j)").unsqueeze(1), AH, GRID, NA_ROW))

        def keep_raw(g, done):
            return on(act, done, dve.now()).activation(before[g][:, :, :].rearrange("p a b -> p (a b)"),
                                                       s.banks[g][:, :], ACT.Copy)

        def silu_steps(first, conv):
            left = s.block_no.at

            def tile(c):
                def step():
                    raw, y = before[c // 2][:, c % 2, :], ybuf[:, ds(first + c, 1), :].rearrange("p a b -> p (a b)")
                    x, d = raw, (s.evacuated[c // 2], left)
                    if conv:
                        if c == 0:
                            d = dve.done(on(dve, d).tensor_copy(filt_w[:, :, :], filt_rows[:, :, ds(first, 4)]))
                        d = dve.done(on(dve, d, (s.evacuated[c // 2], left), act.now()).tensor_scalar(
                            filt[:, :], raw, filt_w[:, 3, c:c + 1], None, ALU.mult))
                        for shift in range(1, 4):
                            o = filt[:, shift:T]
                            d = dve.done(on(dve, d).scalar_tensor_tensor(
                                out=o, in0=raw[:, 0:T - shift], scalar=filt_w[:, 3 - shift, c:c + 1], in1=o,
                                op0=ALU.mult, op1=ALU.add))
                        x = filt[:, :]
                    a = act.done(on(act, d, dve.now()).activation(half_tanh[:, :], x, ACT.Tanh, scale=0.5))
                    dve.done(on(dve, a).scalar_tensor_tensor(out=y, in0=half_tanh[:, :], scalar=1.0, in1=x,
                                                             op0=ALU.add, op1=ALU.mult))
                return step
            return [tile(c) for c in range(4)]

        w_in = w["w_in"]
        run(s.block(columns(w_in, 0), operand, True, keep_raw))
        with p.loop("qkv", 5) as loop:
            steps = silu_steps(loop.i * 4, True)
            weave(s.block(columns(w_in, (loop.i + 1) * COLS), operand, True, keep_raw), steps, 32)
        weave(s.block(columns(w_in, 6 * COLS), operand, True, keep_raw), silu_steps(20, True), 32)
        weave(s.block(columns(w_in, 7 * COLS), operand, True, keep_raw), silu_steps(24, False), 32)
        for step in silu_steps(28, False):
            step()

        wait(act, tab_stored.now())
        conv_ctx.close()

        ident, ones = p.c("ident"), p.c("ones")
        bank = p.ps[2]
        scal = p.sb("gdn_scalars", [P, GDN_H, 9], ctx=gdn_ctx)
        G_0, BETA_0, HALF_BETA_0, TAIL, DECAY, MINUS_DECAY = 0, 2, 4, 6, 7, 8
        gate = p.sb("gates", [P, 6, NT, GDN_H], ctx=gdn_ctx)
        x, ax, sp_, g, tb, _ = (gate[:, i, :, :] for i in range(6))
        ea = p.sb("exp_a_log", [P, GDN_H], ctx=gdn_ctx)
        p.join()
        for i in range(NT):
            m = pe.engine.transpose(bank[:, i * P:(i + 1) * P], lora[:, 2, i * P:(i + 1) * P], ident)
        turned = pe.done(m)
        ab = bank[:, 0:NT * P].rearrange("p (t c) -> p t c", t=NT)

        def over_tiles(v):
            return bc(v.unsqueeze(1), P, NT, GDN_H)

        dve.done(on(dve, turned).tensor_tensor(x, ab[:, :, 32:40], over_tiles(a_dt[:, 1, :]), ALU.add))
        moved = dve.done(on(dve).tensor_scalar(tb, ab[:, :, 40:48], 0.5, None, ALU.mult))
        dve.done(on(dve).tensor_scalar(ax, x, -1.0, None, ALU.mult))
        d = dve.done(on(dve).tensor_tensor(ax, ax, x, ALU.max))
        act.done(on(act, d).activation(tb, tb, ACT.Tanh))
        act.done(on(act).activation(ea[:, :], a_dt[:, 0, :], ACT.Exp))
        act.done(on(act).activation(ax, ax, ACT.Exp, scale=-1.0))
        a = act.done(on(act).activation(sp_, ax, ACT.Ln, bias=1.0))
        dve.done(on(dve, a).scalar_tensor_tensor(out=sp_, in0=x, scalar=0.0, in1=sp_, op0=ALU.max, op1=ALU.add))
        g_made = dve.done(on(dve).scalar_tensor_tensor(out=g, in0=sp_, scalar=-1.0, in1=over_tiles(ea[:, :]),
                                                       op0=ALU.mult, op1=ALU.mult))
        for i in range(NT):
            put = lambda k, src, *a: dve.done(on(dve).tensor_scalar(scal[:, :, k + i], src, *a))
            dve.done(on(dve).tensor_copy(scal[:, :, G_0 + i], g[:, i, :]))
            put(BETA_0, tb[:, i, :], 0.5, 0.5, ALU.mult, ALU.add)
            put(HALF_BETA_0, tb[:, i, :], 0.25, 0.25, ALU.mult, ALU.add)
        pe_sum = on(pe, g_made, moved)
        pe_sum.matmul(bank[:, 0:8], p.c("le"), g[:, 1, :], start=True, stop=True)
        summed = pe.done(pe_sum.matmul(bank[:, 8:16], p.c("gt"), g[:, 0, :], start=True, stop=True))
        act.done(on(act, summed, dve.now()).activation(scal[:, :, DECAY], bank[:, 0:8], ACT.Exp))
        a = act.done(on(act).activation(scal[:, :, TAIL], bank[:, 8:16], ACT.Exp))
        scalars = dve.done(on(dve, a).tensor_scalar(scal[:, :, MINUS_DECAY], scal[:, :, DECAY], -1.0, None, ALU.mult))
        half_norm = p.sb("half_gdn_norm", [P, 1], ctx=gdn_ctx)
        eps_col = p.sb("gdn_norm_rows", [P, 2, 4], ctx=gdn_ctx)
        dve.done(on(dve).tensor_scalar(half_norm[:, :], pcol("gdn_norm_w"), 0.5, None, ALU.mult))
        dve.done(on(dve).memset(eps_col[:, 0, 0:2], 1.0))
        dve.done(on(dve).memset(eps_col[:, 0, 2:4], GDN_D ** -0.5))

        def gdn_tile(name, *shape):
            return p.sb("gdn_" + name, [P, *shape], ctx=gdn_ctx)

        hs, qkv = gdn_tile("head_scalars", 9), gdn_tile("head_qkv", 3, T)
        le_g, gamma, gm = gdn_tile("le_g", NT, P), gdn_tile("gamma", NT, P), gdn_tile("gamma_masked", NT, 2, P)
        ss, rs = gdn_tile("square_sums", 4), gdn_tile("inverse_norms", 4)
        kq, kb, vb = gdn_tile("kq", 4, P), gdn_tile("k_beta", NT, P), gdn_tile("v_beta", NT, P)
        k_tail, k_T, bq_T = gdn_tile("k_tail", P), gdn_tile("k_T", NT, P), gdn_tile("k_beta_q_T", NT, 2, P)
        ma, lv = gdn_tile("m_a_T", NT, 2, P), gdn_tile("m_level", 2, NT, P)
        xq, yy = gdn_tile("inverse", 2, NT, P), gdn_tile("level_product", NT, P)
        u, st, rr, qs, o = (gdn_tile("u", NT, P), gdn_tile("state", P), gdn_tile("rhs", P), gdn_tile("q_state", P),
                            gdn_tile("o", NT, P))
        sq = gdn_tile("squares", P)
        level = p.c("level").rearrange("p (l i) -> p l i", l=7)
        y4 = ybuf[:, :, :].rearrange("p (k h) t -> p k h t", k=4)

        def two(bank, n=2):
            return bank[:, 0:n * P].rearrange("p (a c) -> p a c", a=n)

        def gdn_head(h, fill):
            b0, b1, b2, b3, b4, b5 = p.ps[2:8]
            fill(2)
            p.join()
            staged = dve.done(on(dve).tensor_copy(hs[:, :], scal[:, ds(h, 1), :].rearrange("p a k -> p (a k)")))
            ready = dve.done(on(dve).tensor_copy(qkv[:, :, :], y4[:, 0:3, ds(h, 1), :].rearrange("p k a t -> p k (a t)")))
            for i in range(NT):
                a = act.done(on(act, staged).activation(le_g[:, i, :], p.c("le"), ACT.Copy, scale=hs[:, G_0 + i:G_0 + i + 1]))
            for i in range(NT):
                m = on(pe, a).matmul(b5[:, i * P:(i + 1) * P], p.c("gt"), le_g[:, i, :], start=True, stop=True)
            summed = pe.done(m)
            for n in range(4):
                m = on(pe, ready).transpose(b0[:, n * P:(n + 1) * P], qkv[:, 1 - n // 2, (n % 2) * P:(n % 2 + 1) * P], ident)
            kq_turned = pe.done(m)
            for n in range(2):
                m = pe.engine.transpose(b1[:, n * P:(n + 1) * P], qkv[:, 2, n * P:(n + 1) * P], ident)
            v_turned = pe.done(m)
            fill(2)
            e = act.done(on(act, summed).activation(gamma[:, :, :], two(b5), ACT.Exp))
            gm_made = pool.done(on(pool, e).tensor_tensor(
                gm[:, :, :, :], bc(gamma[:, :, :].unsqueeze(2), P, NT, 2, P),
                bc(p.c("gdn_mask").rearrange("p (k c) -> p k c", k=2).unsqueeze(1), P, NT, 2, P), ALU.mult))
            for n in range(4):
                a = act.done(on(act, kq_turned).activation(sq[:, :], b0[:, n * P:(n + 1) * P], ACT.Square,
                                                           accum_out=ss[:, n:n + 1]))
            d = dve.done(on(dve, a).tensor_scalar(ss[:, :], ss[:, :], 4e-6, None, ALU.add))
            pool.done(on(pool, d).tensor_tensor(rs[:, :], ss[:, :], p.minus_half[:, 0:4], ALU.pow))
            r = pool.done(on(pool).tensor_tensor(rs[:, :], rs[:, :], eps_col[:, 0, :], ALU.mult))
            fill(2)
            vb_made = dve.done(on(dve, v_turned).tensor_tensor(
                vb[:, :, :], two(b1), bc(hs[:, HALF_BETA_0:HALF_BETA_0 + 2].unsqueeze(2), P, NT, P), ALU.mult))
            kq_made = dve.done(on(dve, r).tensor_tensor(kq[:, :, :], two(b0, 4), bc(rs[:, :].unsqueeze(2), P, 4, P), ALU.mult))
            kb_made = dve.done(on(dve).tensor_tensor(
                kb[:, :, :], kq[:, 0:2, :], bc(hs[:, BETA_0:BETA_0 + 2].unsqueeze(2), P, NT, P), ALU.mult))
            tail = act.done(on(act, kq_made).activation(k_tail[:, :], kq[:, 0, :], ACT.Copy, scale=hs[:, TAIL:TAIL + 1]))
            fill(1)
            for n in range(4):
                m = on(pe, kq_made).transpose(b2[:, n * P:(n + 1) * P], kq[:, n, :], ident)
            kq_back = pe.done(m)
            for n in range(2):
                m = on(pe, kb_made).transpose(b3[:, n * P:(n + 1) * P], kb[:, n, :], ident)
            kb_back = pe.done(m)
            act.done(on(act, kq_back).activation(k_T[:, :, :], two(b2), ACT.Copy))
            act.done(on(act).activation(bq_T[:, :, 1, :], b2[:, 2 * P:4 * P].rearrange("p (a c) -> p a c", a=2), ACT.Copy))
            a = act.done(on(act, kb_back).activation(bq_T[:, :, 0, :], two(b3), ACT.Copy))
            fill(2)
            for i in range(NT):
                m = on(pe, a).matmul(b4[:, i * 2 * P:(i + 1) * 2 * P], k_T[:, i, :],
                                     bq_T[:, i, :, :].rearrange("p a c -> p (a c)"), start=True, stop=True)
            gram = pe.done(m)
            ma_made = dve.done(on(dve, gram, gm_made).tensor_tensor(
                ma[:, :, :, :].rearrange("p a k c -> p (a k c)"), b4[:, :], gm[:, :, :, :].rearrange("p a k c -> p (a k c)"),
                ALU.mult))
            m_T = ma[:, :, 0, :]

            def at_level(l):
                return bc(level[:, l, :].unsqueeze(1), P, NT, P)

            lv_made = pool.done(on(pool, ma_made).tensor_tensor(lv[:, 1, :, :], m_T, at_level(1), ALU.mult))
            dve.done(on(dve).tensor_tensor(lv[:, 0, :, :], m_T, at_level(0), ALU.mult))
            q_made = dve.done(on(dve).tensor_tensor(xq[:, 1, :, :], bc(ident.unsqueeze(1), P, NT, P), lv[:, 0, :, :], ALU.subtract))
            for i in range(NT):
                m = on(pe, q_made).transpose(b0[:, i * P:(i + 1) * P], xq[:, 1, i, :], ident)
            x_made = act.done(on(act, pe.done(m)).activation(xq[:, 0, :, :], two(b0), ACT.Copy))
            for l in range(1, 7):
                for i in range(NT):
                    m = on(pe, lv_made, x_made, q_made).matmul(b1[:, i * P:(i + 1) * P], lv[:, l % 2, i, :], xq[:, 0, i, :],
                                                       start=True, stop=True)
                y_done = pe.done(m)
                if l < 6:
                    lv_made = pool.done(on(pool, y_done, q_made).tensor_tensor(lv[:, (l + 1) % 2, :, :], m_T, at_level(l + 1), ALU.mult))
                fill(2)
                y_made = act.done(on(act, y_done).activation(yy[:, :, :], two(b1), ACT.Copy))
                lo = 1 if l == 6 else 0
                for i in range(NT):
                    if not lo:
                        on(pe, y_made).matmul(b2[:, i * P:(i + 1) * P], xq[:, 1, i, :], yy[:, i, :], start=True, stop=True)
                    m = on(pe, y_made).matmul(b2[:, (2 + i) * P:(3 + i) * P], yy[:, i, :], xq[:, 1, i, :], start=True, stop=True)
                z_done = pe.done(m)
                q_made = x_made = dve.done(on(dve, z_done).tensor_tensor(
                    xq[:, lo:2, :, :].rearrange("p a b c -> p (a b c)"), xq[:, lo:2, :, :].rearrange("p a b c -> p (a b c)"),
                    b2[:, lo * 2 * P:4 * P], ALU.subtract))
                fill(2 if l < 6 else 1)
            m = pe.done(on(pe, q_made, vb_made).matmul(b3[:, 0:P], xq[:, 1, 0, :], vb[:, 0, :], start=True, stop=True))
            u0 = act.done(on(act, m).activation(u[:, 0, :], b3[:, 0:P], ACT.Copy))
            m = pe.done(on(pe, u0, tail).matmul(b4[:, 0:P], k_tail[:, :], u[:, 0, :], start=True, stop=True))
            pe.engine.matmul(b5[:, 0:P], ma[:, 0, 1, :], u[:, 0, :], start=True, stop=True)
            s_made = act.done(on(act, m).activation(st[:, :], b4[:, 0:P], ACT.Copy))
            fill(1)
            m = pe.done(on(pe, s_made).matmul(b3[:, 0:P], bq_T[:, 1, 0, :], st[:, :], start=True, stop=True))
            m2 = pe.done(pe.engine.matmul(b4[:, 0:P], bq_T[:, 1, 1, :], st[:, :], start=True, stop=True))
            r_made = dve.done(on(dve, m).scalar_tensor_tensor(out=rr[:, :], in0=b3[:, 0:P], scalar=hs[:, MINUS_DECAY:MINUS_DECAY + 1],
                                                              in1=vb[:, 1, :], op0=ALU.mult, op1=ALU.add))
            qs_made = act.done(on(act, m2).activation(qs[:, :], b4[:, 0:P], ACT.Copy, scale=hs[:, DECAY:DECAY + 1]))
            fill(1)
            m = pe.done(on(pe, r_made).matmul(b3[:, 0:P], xq[:, 1, 1, :], rr[:, :], start=True, stop=True))
            u1 = act.done(on(act, m).activation(u[:, 1, :], b3[:, 0:P], ACT.Copy))
            fill(1)
            m = pe.done(on(pe, u1).matmul(b5[:, P:2 * P], ma[:, 1, 1, :], u[:, 1, :], start=True, stop=True))
            dve.done(on(dve, m).tensor_copy(o[:, 0, :], b5[:, 0:P]))
            o_made = dve.done(on(dve, qs_made).tensor_tensor(o[:, 1, :], b5[:, P:2 * P], qs[:, :], ALU.add))
            for i in range(NT):
                a = act.done(on(act, o_made).activation(sq[:, :], o[:, i, :], ACT.Square, accum_out=ss[:, i:i + 1]))
            d = dve.done(on(dve, a).tensor_scalar(ss[:, 0:2], ss[:, 0:2], 1.0 / GDN_D, NORM_EPS, ALU.mult, ALU.add))
            r = pool.done(on(pool, d).tensor_tensor(rs[:, 0:2], ss[:, 0:2], p.minus_half[:, 0:2], ALU.pow))
            fill(2)
            d = dve.done(on(dve, r).tensor_tensor(o[:, :, :], o[:, :, :], bc(rs[:, 0:2].unsqueeze(2), P, NT, P), ALU.mult))
            for i in range(NT):
                m = on(pe, d).transpose(b0[:, i * P:(i + 1) * P], o[:, i, :], ident)
            m = pe.done(m)
            fill(1)
            dve.done(on(dve, m).scalar_tensor_tensor(
                out=mixg[:, ds(h, 1), :].rearrange("p a t -> p (a t)"), in0=b0[:, 0:T], scalar=half_norm[:, 0:1],
                in1=y4[:, 3, ds(h, 1), :].rearrange("p a t -> p (a t)"), op0=ALU.mult, op1=ALU.mult))
            fill.finish()

        def keep_rwkv(first):
            def read(g, done):
                return on(act, done).activation(rbuf[:, ds(first + 2 * g, 2), :].rearrange("p a b -> p (a b)"),
                                                s.banks[g][:, :], ACT.Copy)
            return read

        p.join()
        with p.loop("gdn_rwkv_columns", 6) as loop:
            gdn_head(loop.i, Filler(s.block(columns(w_in, GDN_COLS + loop.i * COLS), operand, True,
                                            keep_rwkv(loop.i * 4), last=False)))
        with p.loop("gdn", 2) as loop:
            gdn_head(loop.i + 6, Filler())
        gdn_ctx.close()
        k_store = nc.dram_tensor("k_store", (KT, P, T), F32, kind="Internal").ap()
        v_store = nc.dram_tensor("v_store", (P, NT, D), F32, kind="Internal").ap()
        load_m = p.dma_sem("mem_arrived")
        rw_ctx = mix_ctx.enter_context(ExitStack())

        def rw_tile(name, *shape):
            return p.sb("rw_" + name, [P, *shape], ctx=rw_ctx)

        rp = rw_tile("pair_columns", RW_PAIRS, 14)
        (HALF_W0, HALF_A0, K_K, K_A, ONE_K_A, R_K, LN_W, LN_B) = range(8)
        MU, ONE_MU = 8, 11
        w_small, w_gate, w_gate2 = rw_tile("w2_a2", P), rw_tile("g2", P), rw_tile("g2_end", P)
        lo = rw_tile("lora_shifted", 3, T)
        one_mu = rw_tile("one_minus_mu", 4)
        mem_ctx = rw_ctx.enter_context(ExitStack())
        mem_nat = p.sb("mem", [P, NT, D], ctx=mem_ctx)
        p.join(act)
        mem_in = p.dma(act, load_m, mem_nat[:, :, :], t["mem"][0].rearrange("(t p) d -> p t d", p=P))
        p.join()

        def pair_cols(name, n=8, at=0):
            a = PAR[name][0] + at
            return par[:, a:a + n]

        def setp(k, src, a=1.0, b=0.0):
            return dve.done(on(dve).tensor_scalar(rp[:, :, k], src, a, b, ALU.mult, ALU.add))

        setp(HALF_W0, pair_cols("rwkv_w0"), 0.5)
        setp(HALF_A0, pair_cols("rwkv_a0"), 0.5)
        setp(K_K, pair_cols("rwkv_k_k"))
        setp(K_A, pair_cols("rwkv_k_a"))
        setp(ONE_K_A, pair_cols("rwkv_k_a"), -1.0, 1.0)
        setp(R_K, pair_cols("rwkv_r_k"))
        setp(LN_W, pair_cols("rwkv_ln_w"))
        setp(LN_B, pair_cols("rwkv_ln_b"))
        for k in range(3):
            setp(MU + k, pair_cols("mu", 8, 8 * k))
            setp(ONE_MU + k, pair_cols("mu", 8, 8 * k), -1.0, 1.0)
        mu_l = par[:, PAR["mu_lora"][0]:PAR["mu_lora"][0] + 3]
        dve.done(on(dve).tensor_scalar(one_mu[:, 0:3], mu_l, -1.0, 1.0, ALU.mult, ALU.add))

        def shifted(out, y, mu, keep):
            dve.done(on(dve).tensor_scalar(out, y, keep, None, ALU.mult))
            return dve.done(on(dve).scalar_tensor_tensor(out=out[:, 1:T], in0=y[:, 0:T - 1], scalar=mu,
                                                         in1=out[:, 1:T], op0=ALU.mult, op1=ALU.add))

        for k in range(3):
            d = shifted(lo[:, k, :], lora[:, k, :], mu_l[:, k:k + 1], one_mu[:, k:k + 1])
        act.done(on(act, d).activation(lo[0:64, 0, :], lo[0:64, 0, :], ACT.Tanh))
        for part in (lo[:, 1, :], lo[0:32, 2, :]):
            a = act.done(on(act).activation(part, part, ACT.Tanh, scale=0.5))
            d = dve.done(on(dve, a).tensor_scalar(part, part, 0.5, 0.5, ALU.mult, ALU.add))
        free = s.last_used()
        mem_ready = norm_to_operand(p, mem_nat, NORM_EPS, lambda ct: pcol("norm_mem", ct), operand,
                                    after=(mem_in,), free=(free,))
        p.join()
        mem_ctx.close()

        pst = rw_tile("columns", 14)
        rkv = rw_tile("shifted_rkv", 3, T)
        th_w, th_a, gate_T = rw_tile("tanh_w", T), rw_tile("tanh_a", T), rw_tile("gate", T)
        cum, e_in, e_out, e_ex = rw_tile("log_decay", T), rw_tile("exp_in", T), rw_tile("exp_out", T), rw_tile("exp_before", T)
        e_state = rw_tile("state_decay", 4)
        k2, kk, ka = rw_tile("k_scaled", T), rw_tile("k_unit", T), rw_tile("k_unit_a", T)
        sqr, bv = rw_tile("k_squares", T), rw_tile("bonus_v", T)
        rs4, ss4 = rw_tile("inverse_norms", 4), rw_tile("square_sums", 4)
        rsb = rw_tile("inverse_norms_wide", NT, P)
        ar, b_T, k_T = rw_tile("a_r_T", NT, 2, P), rw_tile("b_T", T), rw_tile("kd_T", T)
        vb_n, ka_n = rw_tile("v_b_natural", 4, P), rw_tile("k_a_natural", 4, P)
        gr, lvr = rw_tile("grams_T", 4, 4, P), rw_tile("m_level", 2, 4, P)
        xr, qr, yr = rw_tile("inverse", 4, P), rw_tile("inverse_T", 4, P), rw_tile("level_product", 4, P)
        nv, ur, xa_T = rw_tile("n_v", 4, RW_D), rw_tile("u", 4, RW_D), rw_tile("inverse_a_T", T)
        zs = rw_tile("states", 4, P)
        orw, osq = rw_tile("o", 4, RW_D), rw_tile("o_squares", 4, RW_D)
        stat = rw_tile("o_stats", 4, 4)
        kv_out = [rw_tile(f"kv_out{g}", COLS) for g in range(2)]
        small = [p.dma_sem("small_weights_arrived")]
        kv_sem = [p.dma_sem(f"kv_stored{g}") for g in range(2)]
        dve.done(on(dve).memset(zs[:, 0, :], 0.0))
        dve.done(on(dve).memset(w_gate2[:, :], 0.0))
        DECAY_SCALE = -0.5 * math.exp(-0.5)

        def u_of(rows, i):
            return ur[rows, :, :].rearrange("p (a t) c -> p t a c", a=2)[:, i, :, :]

        def heads2(ap):
            return ap.rearrange("p (a c) -> p a c", a=2)

        def sys4(bank):
            return bank[:, :].rearrange("p (s c) -> p s c", s=4)

        def rwkv_pair(q, fill):
            b0, b1, b2, b3, b4, b5 = p.ps[2:8]
            fill(2)
            p.join()
            wait(act, pe.now())
            for dst, src in ((w_small[0:64, :], t["rwkv_w2"][0, :, ds(q * P, P)]), (w_small[64:128, :], t["rwkv_a2"][0, :, ds(q * P, P)]),
                             (w_gate[:, :], t["rwkv_g2"][0, 0:P, ds(q * P, P)]), (w_gate2[0:32, :], t["rwkv_g2"][0, P:P + 32, ds(q * P, P)])):
                small_in = p.dma(act, small[0], dst, src)
            dve.done(on(dve).tensor_copy(pst[:, :], rp[:, ds(q, 1), :].rearrange("p a k -> p (a k)")))
            col = lambda k: pst[:, k:k + 1]
            for k in range(3):
                d = shifted(rkv[:, k, :], rbuf[:, ds(q + 8 * k, 1), :].rearrange("p a t -> p (a t)"), col(MU + k), col(ONE_MU + k))
                if k == 1:
                    rk_in = d
            v_in = d
            r_, k_, v_ = (rkv[:, k, :] for k in range(3))
            pe_in = on(pe, small_in)
            w_done = pe.done(pe_in.matmul(b0[:, 0:T], w_small[0:64, :], lo[0:64, 0, :], start=True, stop=True))
            a_done = pe.done(pe_in.matmul(b1[:, 0:T], w_small[64:128, :], lo[64:128, 0, :], start=True, stop=True))
            pe_in.matmul(b2[:, 0:T], w_gate[:, :], lo[:, 1, :], start=True, stop=False)
            g_done = pe.done(pe_in.matmul(b2[:, 0:T], w_gate2[:, :], lo[:, 2, :], start=False, stop=True))
            tw = act.done(on(act, w_done, rk_in).activation(th_w[:, :], b0[:, 0:T], ACT.Tanh, scale=0.5, bias=col(HALF_W0)))
            ta = act.done(on(act, a_done).activation(th_a[:, :], b1[:, 0:T], ACT.Tanh, scale=0.5, bias=col(HALF_A0)))
            gT = act.done(on(act, g_done).activation(gate_T[:, :], b2[:, 0:T], ACT.Copy))
            fill(2)
            d = dve.done(on(dve).tensor_scalar(kk[:, :], k_, col(K_K), None, ALU.mult))
            a = act.done(on(act, d).activation(sqr[:, :], kk[:, :], ACT.Square))
            for i in range(NT):
                m = on(pe, a).matmul(b3[:, 2 * i:2 * i + 2], sqr[:, i * P:(i + 1) * P], p.c("headsel"), start=True, stop=True)
            d = dve.done(on(dve, pe.done(m)).tensor_scalar(ss4[:, :], b3[:, 0:4], 1e-6, None, ALU.add))
            r4 = pool.done(on(pool, d).tensor_tensor(rs4[:, :], ss4[:, :], p.minus_half[:, 0:4], ALU.pow))
            dve.done(on(dve, tw).tensor_scalar(th_w[:, :], th_w[:, :], 1.0, DECAY_SCALE, ALU.add, ALU.mult))
            dve.done(on(dve).tensor_tensor_scan(cum[:, :], p.c("reset"), th_w[:, :], 0.0, ALU.mult, ALU.add))
            c4 = cum[:, :].rearrange("p (c t) -> p c t", c=4)
            mids = dve.done(on(dve).tensor_copy(stat[:, 0, :], c4[:, :, RW_C // 2 - 1]))
            dve.done(on(dve).tensor_tensor(c4, c4, bc(stat[:, 0, :].unsqueeze(2), P, 4, RW_C), ALU.subtract))
            centred = dve.done(on(dve).tensor_tensor(e_ex[:, :], cum[:, :], th_w[:, :], ALU.subtract))
            ends = dve.done(on(dve).tensor_tensor(e_state[:, 0:3], c4[:, 0:3, RW_C - 1], stat[:, 0, 1:4], ALU.add))
            act.done(on(act, centred).activation(e_in[:, :], cum[:, :], ACT.Exp))
            act.done(on(act).activation(e_out[:, :], cum[:, :], ACT.Exp, scale=-1.0))
            act.done(on(act).activation(e_ex[:, :], e_ex[:, :], ACT.Exp))
            exps = act.done(on(act, ends).activation(e_state[:, 0:3], e_state[:, 0:3], ACT.Exp))
            fill(2)
            dve.done(on(dve, r4).tensor_copy(rsb[:, :, :].rearrange("p t (h c) -> p (t h) c", h=2), bc(rs4[:, :].unsqueeze(2), P, 4, RW_D)))
            wide = dve.now()
            dve.done(on(dve, ta).tensor_scalar(th_a[:, :], th_a[:, :], 0.5, 0.5, ALU.mult, ALU.add))
            dve.done(on(dve).tensor_scalar(k2[:, :], th_a[:, :], col(K_A), col(ONE_K_A), ALU.mult, ALU.add))
            k2_made = dve.done(on(dve).tensor_tensor(k2[:, :], k2[:, :], k_, ALU.mult))
            for i in range(NT):
                m = on(pe, wide).matmul(b3[:, i * P:(i + 1) * P], rsb[:, i, :], ident, start=True, stop=True)
            scale_done = pe.done(m)
            pool.done(on(pool, k2_made, exps).tensor_tensor(k_T[:, :], k2[:, :], e_out[:, :], ALU.mult))
            ar_v = lambda k: ar[:, :, k, :]
            tt = lambda ap: ap.rearrange("p (t c) -> p t c", t=NT)
            pool.done(on(pool).tensor_tensor(ar_v(1), tt(r_), tt(e_in[:, :]), ALU.mult))
            rk_made = dve.done(on(dve).scalar_tensor_tensor(out=bv[:, :], in0=r_, scalar=col(R_K), in1=k2[:, :], op0=ALU.mult, op1=ALU.mult))
            kk_made = dve.done(on(dve, scale_done).tensor_tensor(kk[:, :], kk[:, :], b3[:, 0:T], ALU.mult))
            dve.done(on(dve, exps).scalar_tensor_tensor(out=ar_v(0), in0=tt(kk[:, :]), scalar=-1.0, in1=tt(e_ex[:, :]), op0=ALU.mult, op1=ALU.mult))
            dve.done(on(dve).tensor_tensor(ka[:, :], kk[:, :], th_a[:, :], ALU.mult))
            made = dve.done(on(dve).tensor_tensor(b_T[:, :], ka[:, :], e_out[:, :], ALU.mult))
            made2 = pool.now()
            m = pe.done(on(pe, rk_made).matmul(b4[:, 0:T], p.c("blockones"), bv[:, :], start=True, stop=True))
            bonus = dve.done(on(dve, m).tensor_tensor(bv[:, :], b4[:, 0:T], v_, ALU.mult))
            fill(2)
            wait(pe, made, made2, v_in)
            for n, (x, y) in enumerate(((v_, k_T[:, :]), (b_T[:, :], None))):
                for i in range(NT):
                    pe.engine.transpose(b0[:, (2 * n + i) * P:(2 * n + i + 1) * P], x[:, i * P:(i + 1) * P], ident)
                    src = y[:, i * P:(i + 1) * P] if y is not None else ar[:, i, 0, :]
                    m = pe.engine.transpose(b1[:, (2 * n + i) * P:(2 * n + i + 1) * P], src, ident)
            turned = pe.done(m)
            wait(pe, bonus)
            for a in range(2):
                c = slice(RW_D * a, RW_D * (a + 1))
                for i in range(NT):
                    bank = (b2, b3, b4, b5)[2 * a + i]
                    rhs = ar[c, i, :, :].rearrange("p k t -> p (k t)")
                    pe.engine.matmul(bank[:, 0:2 * P], b_T[c, i * P:(i + 1) * P], rhs, start=True, stop=True)
                    m = pe.engine.matmul(bank[:, 2 * P:4 * P], k_T[c, i * P:(i + 1) * P], rhs, start=True, stop=True)
            gram = pe.done(m)
            act.done(on(act, turned).activation(vb_n[:, :, :], sys4(b0), ACT.Copy))
            nat_made = act.done(on(act).activation(ka_n[:, :, :], sys4(b1), ACT.Copy))
            wait(dve, gram)
            for n in range(4):
                d = dve.done(on(dve).tensor_tensor(gr[:, n, :, :], sys4((b2, b3, b4, b5)[n]),
                                                   p.c("rw_mask").rearrange("p (k c) -> p k c", k=4), ALU.mult))
                if n == 3:
                    grams = d
            fill(3)
            n_T = gr[:, :, 0, :]

            def at_level(l):
                return bc(level[:, l, :].unsqueeze(1), P, 4, P)

            l_made = pool.done(on(pool, grams).tensor_tensor(lvr[:, 1, :, :], n_T, at_level(1), ALU.mult))
            dve.done(on(dve).tensor_tensor(qr[:, :, :], n_T, at_level(0), ALU.mult))
            q_made = dve.done(on(dve).tensor_tensor(qr[:, :, :], qr[:, :, :], bc(ident.unsqueeze(1), P, 4, P), ALU.add))
            for n in range(4):
                m = on(pe, q_made).transpose(b1[:, n * P:(n + 1) * P], qr[:, n, :], ident)
            x_made = act.done(on(act, pe.done(m)).activation(xr[:, :, :], sys4(b1), ACT.Copy))
            for l in range(1, 6):
                for n in range(4):
                    m = on(pe, l_made, x_made, q_made).matmul(b0[:, n * P:(n + 1) * P], lvr[:, l % 2, n, :], xr[:, n, :], start=True, stop=True)
                y_done = pe.done(m)
                if l < 5:
                    l_made = pool.done(on(pool, y_done).tensor_tensor(lvr[:, (l + 1) % 2, :, :], n_T, at_level(l + 1), ALU.mult))
                fill(2)
                y_made = act.done(on(act, y_done).activation(yr[:, :, :], sys4(b0), ACT.Copy))
                if l < 5:
                    for n in range(4):
                        m = on(pe, y_made).matmul(b1[:, n * P:(n + 1) * P], qr[:, n, :], yr[:, n, :], start=True, stop=True)
                    z_done = pe.done(m)
                for n in range(4):
                    m = on(pe, y_made).matmul(b2[:, n * P:(n + 1) * P], yr[:, n, :], qr[:, n, :], start=True, stop=True)
                zt_done = pe.done(m)
                if l < 5:
                    x_made = dve.done(on(dve, z_done).tensor_tensor(xr[:, :, :], xr[:, :, :], sys4(b1), ALU.add))
                q_made = dve.done(on(dve, zt_done).tensor_tensor(qr[:, :, :], qr[:, :, :], sys4(b2), ALU.add))
                fill(2)
            wait(pe, q_made, nat_made)
            for n in range(4):
                a, i = divmod(n, 2)
                m = pe.engine.matmul(b3[:, n * RW_D:(n + 1) * RW_D], gr[:, n, 2, :], vb_n[:, i, a * RW_D:(a + 1) * RW_D], start=True, stop=True)
            nv_done = pe.done(m)
            for n in range(4):
                a, i = divmod(n, 2)
                c = slice(RW_D * a, RW_D * (a + 1))
                m = pe.engine.matmul(b5[c, i * P:(i + 1) * P], ka_n[:, 2 + i, c], qr[:, n, :], start=True, stop=True)
            xa_done = pe.done(m)
            nv_made = act.done(on(act, nv_done).activation(nv[:, :, :], b3[:, 0:4 * RW_D].rearrange("p (s c) -> p s c", s=4), ACT.Copy))
            for n in range(4):
                m = on(pe, nv_made).matmul(b4[:, n * RW_D:(n + 1) * RW_D], qr[:, n, :], nv[:, n, :], start=True, stop=True)
            uv_done = pe.done(m)
            act.done(on(act, xa_done).activation(xa_T[:, :], b5[:, 0:T], ACT.Copy))
            u_made = act.done(on(act, uv_done).activation(ur[:, :, :], b4[:, 0:4 * RW_D].rearrange("p (s c) -> p s c", s=4), ACT.Copy))
            fill(1)
            for chunk in range(4):
                i, r0 = chunk // 2, RW_C * (chunk % 2)
                rows = slice(r0, r0 + RW_C)
                if chunk:
                    m = on(pe, z_made, u_made).matmul(b1[rows, 0:P], xa_T[:, chunk * RW_C:(chunk + 1) * RW_C], zs[:, chunk, :],
                                                      start=True, stop=True)
                    u_made = dve.done(on(dve, pe.done(m)).tensor_tensor(u_of(rows, i), u_of(rows, i), heads2(b1[rows, 0:P]), ALU.add))
                if chunk < 3:
                    on(pe, u_made).matmul(b0[:, 0:P], ka_n[rows, i, :], vb_n[rows, i, :], start=True, stop=False)
                    m = pe.engine.matmul(b0[:, 0:P], vb_n[rows, 2 + i, :], u_of(rows, i), start=False, stop=True)
                    dve.done(on(dve, pe.done(m)).tensor_tensor(zs[:, chunk + 1, :], zs[:, chunk, :], b0[:, 0:P], ALU.add))
                    z_made = dve.done(on(dve, exps).scalar_tensor_tensor(
                        out=zs[:, chunk + 1, :], in0=zs[:, chunk + 1, :], scalar=e_state[:, chunk:chunk + 1], in1=p.c("blockones"),
                        op0=ALU.mult, op1=ALU.mult))
                fill(1)
            wait(pe, u_made, z_made)
            for n in range(4):
                a, i = divmod(n, 2)
                c = slice(RW_D * a, RW_D * (a + 1))
                o_at = b5[:, n * RW_D:(n + 1) * RW_D]
                pe.engine.matmul(o_at, gr[:, n, 3, :], vb_n[:, i, c], start=True, stop=False, skip_group_check=True)
                m = pe.engine.matmul(o_at, gr[:, n, 1, :], ur[:, n, :], start=False, stop=True, skip_group_check=True)
            within = pe.done(m)
            for chunk in range(4):
                i, r0 = chunk // 2, RW_C * (chunk % 2)
                m = pe.engine.matmul(b3[r0:r0 + RW_C, i * P:(i + 1) * P], ar[:, i, 1, r0:r0 + RW_C], zs[:, chunk, :],
                                     start=True, stop=True)
            across = pe.done(m)
            fill(1)
            d = act.done(on(act, within).activation(orw[:, :, :], b5[:, 0:4 * RW_D].rearrange("p (s c) -> p s c", s=4), ACT.Copy))
            o_at = orw[:, :, :].rearrange("p (a t) c -> p t a c", a=2)
            dve.done(on(dve, across, d).tensor_tensor(o_at, o_at, b3[:, 0:2 * P].rearrange("p (t a c) -> p t a c", t=2, a=2), ALU.add))
            dve.done(on(dve).tensor_reduce(stat[:, 1, :], orw[:, :, :], AX.X, ALU.add))
            dve.done(on(dve).tensor_scalar(stat[:, 1, :], stat[:, 1, :], 1.0 / RW_D, None, ALU.mult))
            d = dve.done(on(dve).tensor_tensor(orw[:, :, :], orw[:, :, :], bc(stat[:, 1, :].unsqueeze(2), P, 4, RW_D), ALU.subtract))
            a = act.done(on(act, d).activation(osq[:, :, :], orw[:, :, :], ACT.Square))
            dve.done(on(dve, a).tensor_reduce(stat[:, 2, :], osq[:, :, :], AX.X, ALU.add))
            d = dve.done(on(dve).tensor_scalar(stat[:, 2, :], stat[:, 2, :], 1.0 / RW_D, RW_EPS, ALU.mult, ALU.add))
            r = pool.done(on(pool, d).tensor_tensor(stat[:, 3, :], stat[:, 2, :], p.minus_half[:, 0:4], ALU.pow))
            fill(2)
            by_tile = orw[:, :, :].rearrange("p (a t) c -> p t a c", a=2)
            d = dve.done(on(dve, r).tensor_tensor(osq[:, :, :].rearrange("p (t a) c -> p t a c", a=2), by_tile,
                                                  bc(stat[:, 3, :].rearrange("p (a t) -> p t a", a=2).unsqueeze(3), P, 2, 2, RW_D), ALU.mult))
            for i in range(NT):
                m = on(pe, d).transpose(b0[:, i * P:(i + 1) * P], osq[:, 2 * i:2 * i + 2, :].rearrange("p a c -> p (a c)"), ident)
            fill(1)
            dve.done(on(dve, pe.done(m)).tensor_scalar(sqr[:, :], b0[:, 0:T], col(LN_W), col(LN_B), ALU.mult, ALU.add))
            dve.done(on(dve).tensor_tensor(sqr[:, :], sqr[:, :], bv[:, :], ALU.add))
            dve.done(on(dve, gT).tensor_tensor(rbuf[:, ds(q, 1), :].rearrange("p a t -> p (a t)"), sqr[:, :], gate_T[:, :], ALU.mult))
            fill.finish()

        def keep_kv(store_of):
            def read(g, done):
                wait(act, (kv_sem[g].sem, kv_sem[g].at))
                m = on(act, done).activation(kv_out[g][:, :], s.banks[g][:, :], ACT.Copy)
                return m
            return read

        def kv_stores(store_of):
            for g in range(2):
                wait(act, (s.evacuated[g], s.block_no.at))
                p.dma(act, kv_sem[g], store_of(g), kv_out[g][:, :])

        wait(pe, mem_ready)
        with p.loop("rwkv_k", 4) as loop:
            rwkv_pair(loop.i, Filler(s.block(columns(w["xattn_wk"], loop.i * COLS), operand, True, keep_kv(None))))
            kv_stores(lambda g: k_store[ds(loop.i * 4 + 2 * g, 2), :, :].rearrange("a p t -> p a t"))
        with p.loop("rwkv_v", 4) as loop:
            rwkv_pair(loop.i + 4, Filler(s.block(columns(w["xattn_wv"], loop.i * COLS), operand, False, keep_kv(None))))
            kv_stores(lambda g: v_store[:, g, ds(loop.i * COLS, COLS)])
        x_free = s.last_used()
        split_T(mixg[:, :, :], 0, (dve.now(),), (x_free,))
        mixed = split_T(rbuf[:, 0:GDN_H, :], GDN_H, (dve.now(),), ())
        rw_ctx.close()
        p.join()
        mix_ctx.close()
        h = p.sb("h", [P, NT, D])
        h_in = p.dma(act, load_x, h[:, :, :], x_tok)

        def add_to_h(first, scale=None):
            def read(g, done):
                wait(dve, h_in, (s.evacuated[g], s.block_no.at + (-1)))
                part = h[:, g, ds(first, COLS)]
                if scale is None:
                    return on(dve, done).tensor_tensor(part, part, s.banks[g][:, :], ALU.add)
                return on(dve, done).scalar_tensor_tensor(out=part, in0=part, scalar=scale, in1=s.banks[g][:, :],
                                                          op0=ALU.mult, op1=ALU.add)
            return read

        def h_done():
            return [(s.evacuated[g], s.block_no.at) for g in range(NT)]

        wait(pe, mixed)
        with p.loop("w_out", D // COLS) as loop:
            run(s.block(columns(w["w_out"], loop.i * COLS), operand, False, add_to_h(loop.i * COLS)))
        xa_ctx = ctx.enter_context(ExitStack())

        def xa_tile(name, *shape):
            return p.sb("xa_" + name, [P, *shape], ctx=xa_ctx)

        xk, xv, xo = xa_tile("k_T", KT, T), xa_tile("v", NT, D), xa_tile("o_T", KT, T)
        qh, vh = xa_tile("head_q_T", XD // P, T), xa_tile("head_v", NT, XD)
        e, e_T = xa_tile("weights", NT, T), xa_tile("weights_T", NT, T)
        mx, den = xa_tile("max", NT), xa_tile("sum", NT)
        load_kv = p.dma_sem("kv_arrived")
        p.join(act)
        wait(act, *[k.now() for k in kv_sem])
        p.dma(act, load_kv, xk[:, :, :], k_store.rearrange("k p t -> p k t"))
        kv_in = p.dma(act, load_kv, xv[:, :, :], v_store)
        q_ready = norm_to_operand(p, h, NORM_EPS, lambda ct: pcol("norm_xattn", ct), operand, after=h_done(),
                                  free=(s.last_used(),))

        def keep_q(g, done):
            return on(act, done).activation(qh[:, 2 * g:2 * g + 2, :].rearrange("p a b -> p (a b)"),
                                            s.banks[g][:, :], ACT.Copy)

        def cross_head(n):
            b0, b1, b2, b3 = p.ps[2:6]
            left = s.block_no.at
            tok = {}

            def scores():
                wait(pe, kv_in, *[(s.evacuated[g], left) for g in range(2)], *[x.now() for x in (act, dve)])
                for i in range(NT):
                    for c in range(XD // P):
                        m = pe.engine.matmul(b0[:, i * T:(i + 1) * T], qh[:, c, i * P:(i + 1) * P],
                                             xk[:, ds(n * (XD // P) + c, 1), :].rearrange("p a t -> p (a t)"),
                                             start=c == 0, stop=c == XD // P - 1)
                tok["s"] = pe.done(m)
                tok["v"] = dve.done(on(dve, kv_in, pe.now()).tensor_copy(vh[:, :, :], xv[:, :, ds(n * XD, XD)]))

            def maxima():
                s2 = b0[:, :].rearrange("p (t m) -> p t m", t=NT)
                dve.done(on(dve, tok["s"]).tensor_reduce(mx[:, :], s2, AX.X, ALU.max))
                tok["m"] = dve.done(on(dve).tensor_scalar(mx[:, :], mx[:, :], -XD ** -0.5, None, ALU.mult))
                for i in range(NT):
                    tok["e"] = act.done(on(act, tok["m"]).activation(
                        e[:, i, :], b0[:, i * T:(i + 1) * T], ACT.Exp, scale=XD ** -0.5, bias=mx[:, i:i + 1],
                        accum_out=den[:, i:i + 1]))

            def normalise():
                dve.done(on(dve, tok["e"]).reciprocal(den[:, :], den[:, :]))
                d = dve.done(on(dve).tensor_tensor(e[:, :, :], e[:, :, :], bc(den[:, :].unsqueeze(2), P, NT, T), ALU.mult))
                for i in range(NT):
                    for m_ in range(NT):
                        m = on(pe, d).transpose(b1[:, m_ * T + i * P:m_ * T + (i + 1) * P], e[:, i, m_ * P:(m_ + 1) * P], ident)
                tok["t"] = act.done(on(act, pe.done(m)).activation(e_T[:, :, :].rearrange("p a b -> p (a b)"), b1[:, :], ACT.Copy))

            def values():
                wait(pe, tok["t"], tok["v"])
                for c in range(XD // P):
                    for m_ in range(NT):
                        o = (b2, b3)[c // 2][:, (c % 2) * T:(c % 2 + 1) * T]
                        m = pe.engine.matmul(o, vh[:, m_, c * P:(c + 1) * P], e_T[:, m_, :], start=m_ == 0, stop=m_ == NT - 1)
                tok["o"] = pe.done(m)

            def outputs():
                for c in range(2):
                    act.done(on(act, tok["o"]).activation(
                        xo[:, ds(n * (XD // P) + 2 * c, 2), :].rearrange("p a b -> p (a b)"), (b2, b3)[c][:, :], ACT.Copy))
            return [scores, maxima, normalise, values, outputs]

        wait(pe, q_ready)
        wq = w["xattn_wq"]
        run(s.block(columns(wq, 0), operand, True, keep_q))
        with p.loop("cross_attention", XH - 1) as loop:
            steps = cross_head(loop.i)
            weave(s.block(columns(wq, (loop.i + 1) * COLS), operand, True, keep_q), steps, 32, first=1)
        for step in cross_head(XH - 1):
            step()
        wait(pe, split_T(xo[:, :, :], 0, (act.now(),), (s.last_used(),)))
        with p.loop("xattn_wo", D // COLS) as loop:
            run(s.block(columns(w["xattn_wo"], loop.i * COLS), operand, False, add_to_h(loop.i * COLS)))
        xa_ctx.close()
        mlp_ctx = ctx.enter_context(ExitStack())
        relu = [p.sb(f"mlp_relu{g}", [P, 2, T], ctx=mlp_ctx) for g in range(2)]
        hid = [p.sb("mlp_hidden_" + x, [P, KT, T], F32R, ctx=mlp_ctx) for x in ("head", "rest")]
        p.join()
        wait(pe, norm_to_operand(p, h, NORM_EPS, lambda ct: pcol("norm_mlp", ct), operand, after=h_done(),
                                 free=(s.last_used(),)))

        def keep_relu(g, done):
            return on(act, done, pool.now(), dve.now()).activation(relu[g][:, :, :].rearrange("p a b -> p (a b)"),
                                                                   s.banks[g][:, :], ACT.Relu)

        def square(first):
            def after(g):
                r, at = relu[g][:, :, :], ds(first + 2 * g, 2)
                d = pool.done(on(pool, (s.evacuated[g], s.block_no.at)).tensor_tensor(r, r, r, ALU.mult))
                a = act.done(on(act, d).activation(hid[0][:, at, :], r, ACT.Copy))
                dve.done(on(dve, a).tensor_tensor(hid[1][:, at, :], r, hid[0][:, at, :].bitcast(F32), ALU.subtract))
            return after

        with p.loop("mlp", D_FF // D) as quarter:
            with p.loop("mlp_up", D // COLS) as loop:
                run(s.block(columns(w["mlp_w_up"], quarter.i * D + loop.i * COLS), operand, True, keep_relu,
                            after=square(loop.i * (COLS // P))))
            hid_made = dve.now()
            with p.loop("mlp_down", D // COLS) as loop:
                run(s.block(columns(w["mlp_w_down"], loop.i * COLS, rows=quarter.i * D), hid, False,
                            add_to_h(loop.i * COLS), ready=(hid_made,)))
        mlp_ctx.close()
        p.join()
        fin_ctx = ctx.enter_context(ExitStack())
        fin_gain = p.sb("norm_final_rows", [P, D], ctx=fin_ctx)
        load_r = p.dma_sem("gain_rows_arrived")
        gain_in = p.dma(act, load_r, fin_gain[:, :], t["norm_final"].partition_broadcast(P))
        scaled = norm_scale(p, h_done(), h, NORM_EPS, None)
        for i in range(NT):
            normed = dve.done(on(dve, scaled, gain_in, act.now()).scalar_tensor_tensor(
                out=h[:, i, :], in0=h[:, i, :], scalar=p.rstd[:, i:i + 1], in1=fin_gain[:, :], op0=ALU.mult, op1=ALU.mult))
        x2_ready = to_operand(p, h, lambda i: ident, None, operand, after=(normed,), free=(s.last_used(),))
        fin_ctx.close()

        att_ctx = ctx.enter_context(ExitStack())

        def att_tile(name, *shape):
            return p.sb("att_" + name, [P, *shape], ctx=att_ctx)

        half_w = AH * AD
        halves_ = [dict(qk=att_tile(f"qk_T_{n}", 16, T), v=att_tile(f"v_{n}", NT, half_w), g=att_tile(f"gate_T_{n}", 8, T))
                   for n in "ab"]
        g_tanh = att_tile("gate_tanh", 2, T)
        qs2, ks2, vs2 = att_tile("pair_q_T", T), att_tile("pair_k_T", T), att_tile("pair_v", NT, P)
        sc, sc_T = att_tile("scores", 2, NT, T), att_tile("weights_T", 2, NT, T)
        a_max, a_sum = att_tile("max", 2, NT), att_tile("sum", 2, NT)
        bias_sem = p.dma_sem("pair_bias_arrived")
        p.join()

        def keep_qk(half, first):
            def read(g, done):
                return on(act, done).activation(half["qk"][:, ds(first + 2 * g, 2), :].rearrange("p a b -> p (a b)"),
                                                s.banks[g][:, :], ACT.Copy)
            return read

        def keep_v(half, first):
            def read(g, done):
                return on(act, done).activation(half["v"][:, g, ds(first, COLS)], s.banks[g][:, :], ACT.Copy)
            return read

        def keep_g(half, first):
            def read(g, done):
                x = s.banks[g][:, :].rearrange("p (a t) -> p a t", a=2)
                free = (s.evacuated[1 - g], s.block_no.at + (g - 1))
                a = act.done(on(act, done, free).activation(g_tanh[:, :, :], x, ACT.Tanh, scale=0.5))
                return on(dve, a).scalar_tensor_tensor(out=half["g"][:, ds(first + 2 * g, 2), :], in0=g_tanh[:, :, :],
                                                       scalar=1.0, in1=x, op0=ALU.add, op1=ALU.mult)
            return read

        def t5_bias(n, a, i):
            base = bass.AP(t5_store.tensor, (NT - i) * P - 1, ap=[[P * 2 * T, AH], [2 * T - 1, P], [1, T]])
            return [(slice(0, P), base[ds(2 * n + a, 1), :, :].rearrange("h p j -> (h p) j"))]

        def na_bias(n, a, i):
            parts = []
            for r in range(2):
                at = GRID - 1 + (3 - 2 * i - r) * P
                base = bass.AP(na_store.tensor, at, ap=[[GRID * NA_ROW, AH], [NA_ROW - 1, GRID], [P, 4], [1, GRID]])
                parts.append((slice(GRID * r, GRID * (r + 1)), base[ds(2 * n + a, 1), :, :, :].rearrange("h p r j -> (h p) r j")))
            return parts

        def pair_attention(half, n, bias_of, masked):
            b = p.ps[2:7]
            tok = {}
            tile = lambda x, k: x[:, ds(k, 1), :].rearrange("p a t -> p (a t)")

            def stage():
                wait(act, dve.now(), pe.now())
                for a in range(2):
                    for i in range(NT):
                        for rows, src in bias_of(n, a, i):
                            dst = sc[rows, a, i, :]
                            if masked:
                                dst = dst.rearrange("p (r j) -> p r j", r=4)
                            tok["b"] = p.dma(act, bias_sem, dst, src)
                dve.done(on(dve, pe.now(), act.now()).tensor_copy(qs2[:, :], tile(half["qk"], n)))
                tok["qk"] = dve.done(on(dve).tensor_copy(ks2[:, :], tile(half["qk"], n + 8)))
                tok["v"] = dve.done(on(dve).tensor_copy(vs2[:, :, :], half["v"][:, :, ds(n * P, P)]))

            def scores():
                wait(pe, tok["qk"])
                for a in range(2):
                    c = slice(AD * a, AD * (a + 1))
                    for i in range(NT):
                        m = pe.engine.matmul(b[a][:, i * T:(i + 1) * T], qs2[c, i * P:(i + 1) * P], ks2[c, :], start=True, stop=True)
                    tok["s", a] = pe.done(m)

            def weigh(a):
                def step():
                    x = sc[:, a, :, :]
                    dve.done(on(dve, tok["s", a], tok["b"]).tensor_tensor(x, x, b[a][:, :].rearrange("p (t j) -> p t j", t=NT), ALU.add))
                    if masked:
                        x4 = sc[:, a, :, :].rearrange("p t (r j) -> p (t r) j", j=GRID)
                        dve.done(on(dve).tensor_tensor(x4, x4, bc(p.c("na_mask").unsqueeze(1), P, 4 * NT, GRID), ALU.add))
                    dve.done(on(dve).tensor_reduce(a_max[:, a, :], x, AX.X, ALU.max))
                    m = dve.done(on(dve).tensor_scalar(a_max[:, a, :], a_max[:, a, :], -AD ** -0.5, None, ALU.mult))
                    for i in range(NT):
                        tok["e", a] = act.done(on(act, m).activation(sc[:, a, i, :], sc[:, a, i, :], ACT.Exp, scale=AD ** -0.5,
                                                                     bias=a_max[:, a, i:i + 1], accum_out=a_sum[:, a, i:i + 1]))
                return step

            def normalise(a):
                def step():
                    dve.done(on(dve, tok["e", a]).reciprocal(a_sum[:, a, :], a_sum[:, a, :]))
                    x = sc[:, a, :, :]
                    d = dve.done(on(dve).tensor_tensor(x, x, bc(a_sum[:, a, :].unsqueeze(2), P, NT, T), ALU.mult))
                    wait(pe, d)
                    for i in range(NT):
                        for k in range(NT):
                            m = pe.engine.transpose(b[2 + a][:, k * T + i * P:k * T + (i + 1) * P], sc[:, a, i, k * P:(k + 1) * P], ident)
                    tok["t", a] = act.done(on(act, pe.done(m)).activation(sc_T[:, a, :, :].rearrange("p k t -> p (k t)"), b[2 + a][:, :], ACT.Copy))
                return step

            def values():
                wait(pe, tok["v"], tok["t", 1])
                for a in range(2):
                    c = slice(AD * a, AD * (a + 1))
                    for k in range(NT):
                        m = pe.engine.matmul(b[4][c, 0:T], vs2[:, k, c], sc_T[:, a, k, :], start=k == 0, stop=k == NT - 1)
                dve.done(on(dve, pe.done(m)).scalar_tensor_tensor(
                    out=tile(half["qk"], n), in0=b[4][:, 0:T], scalar=0.5, in1=tile(half["g"], n), op0=ALU.mult, op1=ALU.mult))

            return [stage, scores, weigh(0), weigh(1), normalise(0), normalise(1), values]

        w2 = w["w_in_2"]
        wait(pe, x2_ready)
        KINDS = (("qk", 4, True, keep_qk, COLS // P), ("v", 2, False, keep_v, COLS), ("g", 2, True, keep_g, COLS // P))

        def projections(half, first, name, steps_of=None):
            at = 0
            for kind, n, transposed, keep, step in KINDS:
                with p.loop(name + kind, n) as loop:
                    block = s.block(columns(w2, (loop.i + at) * COLS + first), operand, transposed, keep(half, loop.i * step))
                    if steps_of:
                        weave(block, steps_of(loop.i + at), 32 if transposed else 16, first=1)
                    else:
                        run(block)
                at += n

        projections(halves_[0], 0, "a_")
        projections(halves_[1], 4 * half_w, "b_", lambda n: pair_attention(halves_[0], n, t5_bias, False))
        with p.loop("neighbourhood", AH // 2) as loop:
            for step in pair_attention(halves_[1], loop.i, na_bias, True):
                step()
        for n in range(2):
            y_ready = split_T(halves_[n]["qk"][:, 0:8, :], 8 * n, (dve.now(),), (s.last_used(),))
        p.join()
        att_ctx.close()
        ln_rows = p.sb("ln_rows", [P, 2, D])
        wide = p.sb("ln_wide", [P, NT, D])
        ln_mean = p.sb("ln_mean", [P, NT])
        p.dma(act, load_r, ln_rows[:, 0, :], t["ln_gain_2"][0].partition_broadcast(P))
        ln_in = p.dma(act, load_r, ln_rows[:, 1, :], t["ln_bias_2"][0].partition_broadcast(P))
        with p.loop("w_out_2", D // COLS - 1) as loop:
            run(s.block(columns(w["w_out_2"], loop.i * COLS), operand, False, add_to_h(loop.i * COLS, ALPHA), ready=(y_ready,)))
        run(s.block(columns(w["w_out_2"], D - COLS), operand, False, add_to_h(D - COLS, ALPHA), last=True))
        stored = p.dma_sem("out_stored")
        out_tok = out[0].rearrange("(t p) d -> p t d", p=P)
        for i in range(NT):
            dve.done(on(dve, *h_done()).tensor_reduce(ln_mean[:, i:i + 1], h[:, i, :], AX.X, ALU.add))
            m = dve.done(on(dve).tensor_scalar(ln_mean[:, i:i + 1], ln_mean[:, i:i + 1], -1.0 / D, None, ALU.mult))
            sq = act.done(on(act, m, pe.now()).activation(p.junk[:, :], h[:, i, :], ACT.Square, bias=ln_mean[:, i:i + 1],
                                                          accum_out=p.ss[:, i:i + 1]))
            pool.done(on(pool, sq).tensor_scalar(p.ss[:, 2 + i:3 + i], p.ss[:, i:i + 1], 1.0 / D, LN_EPS, ALU.mult, ALU.add))
            r = pool.done(on(pool).tensor_tensor(p.rstd[:, i:i + 1], p.ss[:, 2 + i:3 + i], p.minus_half[:, 0:1], ALU.pow))
            dve.done(on(dve, r).tensor_scalar(wide[:, i, :], h[:, i, :], ln_mean[:, i:i + 1], p.rstd[:, i:i + 1], ALU.add, ALU.mult))
            for c in range(0, D, COLS):
                c = slice(c, c + COLS)
                x = wide[:, i, c]
                dve.done(on(dve, ln_in).tensor_tensor(x, x, ln_rows[:, 0, c], ALU.mult))
                d = dve.done(on(dve).tensor_tensor(x, x, ln_rows[:, 1, c], ALU.add))
                wait(sp, d)
                p.dma(sp, stored, out_tok[:, i, c], x)
        wait(sp, stored.now())
    return p


def kernel(**inputs):
    import concourse.bacc as bacc
    from concourse.bass_utils import run_bass_kernel_spmd

    arrays = {f"in_{name}_dram": np.ascontiguousarray(a) for name, a in dict(inputs, **constants()).items()}
    plan = {}
    for _ in range(2):
        nc = bacc.Bacc("TRN2", target_bir_lowering=False, num_devices=1)
        t = {name[3:-5]: nc.dram_tensor(name, a.shape, mybir.dt.from_np(a.dtype), kind="ExternalInput").ap()
             for name, a in arrays.items()}
        build_program(nc, t, nc.dram_tensor("out_0_dram", (1, T, D), F32, kind="ExternalOutput").ap(), plan)
    return run_bass_kernel_spmd(nc, [arrays], core_ids=[0]).results[0]["out_0_dram"]
```

```python
import math
from contextlib import ExitStack, contextmanager

import numpy as np

import concourse.bass as bass
from concourse import mybir

F32 = mybir.dt.float32
F32R = mybir.dt.float32r
BF16 = mybir.dt.bfloat16
ALU = mybir.AluOpType
ACT = mybir.ActivationFunctionType
AX = mybir.AxisListType
ds = bass.ds

P = 128
D = 2048
T = 256
NT = T // P
KT = D // P
SLOT_K = 4
COLS = 512
SLOTS = KT // SLOT_K
HALF_K, HALVES, RING = SLOT_K // 2, 2 * SLOTS, 4
NORM_EPS = 1e-6

GDN_H, GDN_D = 8, 128
GDN_W = GDN_H * GDN_D
GDN_COLS = 4 * GDN_W + 2 * GDN_H
RW_H, RW_D, RW_C = 16, 64, 64
RW_W = RW_H * RW_D
RW_PAIRS = RW_H // 2
LORA_W, LORA_A, LORA_G = 64, 64, 160
LORA = LORA_W + LORA_A + LORA_G
LORA_COL = GDN_COLS + 3 * RW_W
RW_EPS = 64e-5
XH, XD = 4, 512
AH, AD = 16, 64
D_FF = 4 * D
LN_EPS = 1e-5
ALPHA = 2.0 ** 0.25
GRID, NA_ROW = 64, 7 * P
NEG = -8e30


def _columns():
    at, out = 0, {}
    for name, n in (("ident", P), ("ones", 2 * P), ("blockones", P), ("le", P), ("gt", P), ("gdn_mask", 2 * P),
                    ("level", 7 * P), ("rw_mask", 4 * P), ("headsel", 2), ("reset", T), ("na_mask", 64)):
        out[name] = (at, n)
        at += n
    return out, at


CONST, N_CONST = _columns()


def _bucket(rel):
    half, exact = 16, 8
    n = np.abs(rel)
    large = exact + (np.log(np.maximum(n, 1) / exact) / np.log(1024 / exact) * (half - exact)).astype(np.int64)
    return (rel > 0) * half + np.where(n < exact, n, np.minimum(large, half - 1))


def constants():
    c = np.zeros((P, N_CONST), np.float32)
    j, i = np.arange(P)[:, None], np.arange(P)[None, :]

    def put(name, a):
        at, n = CONST[name]
        c[:, at:at + n] = a.reshape(P, n)

    put("ident", (i == j) * 1.0)
    put("ones", np.ones((P, 2 * P)))
    put("blockones", (i // RW_D == j // RW_D) * 1.0)
    put("le", (j <= i) * 1.0)
    put("gt", (j > i) * 1.0)
    put("gdn_mask", np.stack([j < i, j <= i], 1) * 1.0)
    put("level", np.stack([((i >> l + 1) == (j >> l + 1)) & ((i >> l) % 2 == 1) & ((j >> l) % 2 == 0)
                           for l in range(7)], 1) * 1.0)
    same = i // RW_C == j // RW_C
    put("rw_mask", np.stack([same & (j < i), same & (j <= i)] * 2, 1) * 1.0)
    put("headsel", (j // RW_D == np.arange(2)[None, :]) * 1.0)
    put("reset", np.broadcast_to(np.arange(T) % RW_C != 0, (P, T)) * 1.0)
    q, k = np.arange(P)[:, None] % 64, np.arange(64)[None, :]
    start = np.clip(q - 8, 0, 48)
    put("na_mask", np.where((k >= start) & (k < start + 16), 0.0, NEG))
    rel = np.arange(512) - 255
    onehot = (_bucket(rel)[None, :] == np.arange(32)[:, None]) * 1.0
    count = (np.abs(rel) <= 64) * 1.0 + (rel % 4 == 0) + (rel % 16 == 0)
    logs = np.where(count > 0, 8.0 * np.log(np.maximum(count, 1)), NEG)
    dil = np.concatenate([onehot, np.broadcast_to(logs, (32, 512))], 1).astype(np.float32)
    return {"consts": c, "dilated": dil}


class Lin:

    def __init__(self, c=0, steps=()):
        self.c, self.steps = c, tuple(steps)

    def __add__(self, n):
        return Lin(self.c + n, self.steps)

    def stepped(self, loop, step):
        return Lin(self.c, self.steps + ((loop, step),))

    def times(self, k):
        return Lin(self.c * k, [(l, s * k) for l, s in self.steps])

    def value(self):
        v, live = self.c, []
        for loop, step in self.steps:
            if loop.closed:
                v += step * (loop.n - 1)
            elif step:
                live.append(loop.i * step)
        for x in live:
            v = x + v
        return v


class Loop:
    def __init__(self, i, n):
        self.i, self.n, self.closed = i, n, False


class Counter:
    def __init__(self, name, sem=None):
        self.name, self.sem, self.at = name, sem, Lin()

    def now(self):
        return self.sem, self.at


class Lane(Counter):

    def __init__(self, nc, ctx, name, engine):
        super().__init__(name, ctx.enter_context(nc.semaphore("done_" + name)))
        self.engine, self.ordered = engine, name in ("scalar", "vector", "gpsimd")

    def done(self, ins):
        ins.then_inc(self.sem, 1)
        self.at = self.at + 1
        return self.sem, self.at


def on(lane, *tokens):
    wait(lane, *tokens, lane.now() if lane.ordered else None)
    return lane.engine


def wait(lane, *tokens):
    latest = {}
    for t in tokens:
        if t is not None:
            key = id(t[0]), t[1].steps
            if key not in latest or latest[key][1].c < t[1].c:
                latest[key] = t
    for sem, at in latest.values():
        if at.c > 0 or at.steps:
            lane.engine.wait_ge(sem, at.value())


class Program:
    def __init__(self, nc, ctx, plan):
        self.nc, self.ctx, self.plan = nc, ctx, plan
        self.pe = Lane(nc, ctx, "tensor", nc.tensor)
        self.act = Lane(nc, ctx, "scalar", nc.scalar)
        self.dve = Lane(nc, ctx, "vector", nc.vector)
        self.pool = Lane(nc, ctx, "gpsimd", nc.gpsimd)
        self.sp = Lane(nc, ctx, "sync", nc.sync)
        self.lanes = [self.pe, self.act, self.dve, self.pool]
        self.counters = list(self.lanes)
        self.n_names = 0

    def sb(self, name, shape, dt=F32, ctx=None):
        return (ctx or self.ctx).enter_context(self.nc.sbuf_tensor(name, shape, dt))

    def counter(self, name, sem=None):
        c = Counter(name, sem)
        self.counters.append(c)
        return c

    def sem(self, name):
        return self.ctx.enter_context(self.nc.semaphore(name))

    def dma_sem(self, name):
        return self.counter(name, self.sem(name))

    def dma(self, lane, counter, out, in_, **kw):
        lane.engine.dma_start(out, in_, **kw).then_inc(counter.sem, 16)
        counter.at = counter.at + 16
        return counter.sem, counter.at

    @contextmanager
    def loop(self, name, n):
        starts = [c.at for c in self.counters]
        with self.nc.Fori(0, n) as i:
            loop = Loop(i, n)
            for c, s in zip(self.counters, starts):
                c.at = s.stepped(loop, self.plan.get((name, c.name), 0))
            yield loop
        loop.closed = True
        for c, s in zip(self.counters, starts):
            gain = c.at.c - s.c
            self.plan[(name, c.name)] = gain
            c.at = s + n * gain

    def join(self, *lanes):
        marks = [x.now() for x in self.lanes]
        for lane in lanes or self.lanes:
            wait(lane, *[m for x, m in zip(self.lanes, marks) if x is not lane])


def bc(ap, *shape):
    return ap.to_broadcast(list(shape))


class Stream:

    def __init__(self, p):
        self.p, nc = p, p.nc
        self.raw = [p.sb(f"weights_raw{j}", [P, SLOT_K, COLS]) for j in range(SLOTS)]
        self.head = [p.sb(f"weights_head{k}", [P, HALF_K, COLS], F32R) for k in range(RING)]
        self.rest = [p.sb(f"weights_rest{k}", [P, HALF_K, COLS], F32R) for k in range(RING)]
        self.arrived = [p.sem(f"weights_arrived{j}") for j in range(SLOTS)]
        self.s_head, self.s_rest, self.s_used = (p.sem("weights_" + x) for x in ("head_made", "rest_made", "used"))
        self.evacuated = [p.sem(f"product_bank{g}_read") for g in range(2)]
        self.banks = [p.ps[0], p.ps[1]]
        self.block_no = p.counter("block")

    def used(self, block, k):
        return self.s_used, block.times(HALVES) + (k + 1)

    def last_used(self):
        return self.used(self.block_no.at + (-1), HALVES - 1)

    def load(self, block, j, parts):
        sp, n = self.p.sp, 0
        if block.c or block.steps:
            wait(sp, (self.s_rest, (block + (-1)).times(HALVES) + (2 * j + 2)))
        for ap in parts:
            w = ap.shape[1]
            sp.engine.dma_start(self.raw[j][:, :, n:n + w], ap.rearrange("(k p) n -> p k n", p=P)) \
                .then_inc(self.arrived[j], 16)
            n += w

    def split(self, block, k, cols=COLS):
        p = self.p
        rows = slice(k % 2 * HALF_K, (k % 2 + 1) * HALF_K)
        raw, head, rest = self.raw[k // 2][:, rows, 0:cols], self.head[k % RING], self.rest[k % RING]
        if k % 2 == 0:
            wait(p.act, (self.arrived[k // 2], block.times(16) + 32))
        if k >= RING:
            wait(p.act, self.used(block, k - RING))
        elif block.c or block.steps:
            wait(p.act, self.used(block + (-1), k + HALVES - RING))
        p.act.engine.activation(head[:, :, 0:cols], raw, ACT.Copy).then_inc(self.s_head, 1)
        wait(p.dve, (self.s_head, block.times(HALVES) + (k + 1)))
        p.dve.engine.tensor_tensor(rest[:, :, 0:cols], raw, head[:, :, 0:cols].bitcast(F32),
                                   ALU.subtract).then_inc(self.s_rest, 1)

    def block(self, source, operand, transposed, read, cols=COLS, last=False, ready=(), late=(), after=None,
              parts=1, first_kt=0):
        p, pe = self.p, self.p.pe
        head_x, rest_x = operand
        block = self.block_no.at
        self.block_no.at = block + 1
        wait(pe, *ready)
        banks = range((cols + 2 * P - 1) // (2 * P)) if transposed else range(NT)
        per_part, part_read = HALVES // parts, {}
        for half in range(HALVES):
            part, first, final = half // per_part, half % per_part == 0, (half + 1) % per_part == 0
            if half % 2 == 0:
                self.load(block, half // 2, source(half // 2))
            wait(pe, (self.s_rest, block.times(HALVES) + (half + 1)), *(late if half == HALVES - 2 else ()))
            head, rest = self.head[half % RING], self.rest[half % RING]
            for g in banks:
                bank = self.banks[g]
                if half == 0 and (block.c or block.steps):
                    wait(pe, (self.evacuated[g], block))
                if first and part:
                    wait(pe, part_read[g])
                ends = range(2 * g, min(2 * g + 2, (cols + P - 1) // P)) if transposed else (g,)
                for c in ends:
                    for k in range(HALF_K):
                        kt = first_kt + half % per_part * HALF_K + k
                        for a in range(3):
                            w = (head, rest, head)[a]
                            x = (head_x, head_x, rest_x)[a]
                            if transposed:
                                w = (head, head, rest)[a]
                                x = (head_x, rest_x, head_x)[a]
                            kw = {"start": first and k == 0 and a == 0 and c == ends[0], "skip_group_check": True,
                                  "stop": final and k == HALF_K - 1 and a == 2}
                            if transposed:
                                o = (c - ends[0]) * T
                                m = pe.engine.matmul(bank[:, o:o + T], w[:, k, c * P:(c + 1) * P], x[:, kt, :], **kw)
                            else:
                                m = pe.engine.matmul(bank[:, :], x[:, kt, g * P:(g + 1) * P], w[:, k, :], **kw)
                    if c == ends[-1]:
                        if g == banks[-1]:
                            m.then_inc(self.s_used, 1)
                            done = self.used(block, half)
                        elif final:
                            done = pe.done(m)
                    yield
                if half == HALVES - 1:
                    (read[part] if parts > 1 else read)(g, done).then_inc(self.evacuated[g], 1)
                elif final:
                    part_read[g] = p.dve.done(read[part](g, done))
            if half + RING < HALVES:
                self.split(block, half + RING, cols)
            elif not last:
                self.split(block + 1, half + RING - HALVES)
        if after:
            for g in banks:
                after(g)

    def start(self, cols):
        for k in range(RING):
            self.split(Lin(), k, cols)


def half_columns(w, first, rows):
    return lambda j: [w[ds(rows + j % 2 * SLOT_K * P, SLOT_K * P), ds(first + j // 2 * COLS, COLS)]]


def run(pieces):
    for _ in pieces:
        pass


FIRST, LEAD = 0.25, 2


def interleave(p, **chains):
    live = [[0, p.plan.get((name, "steps"), 1), name, gen] for name, gen in chains.items()]

    def position(chain):
        if chain[2] in ("k_block", "v_block"):
            return ((chain[0] + 1) / chain[1] - FIRST) / (1 - FIRST)
        return (chain[0] + 1 - LEAD) / chain[1]

    while live:
        chain = min(live, key=position)
        if next(chain[3], live) is live:
            live.remove(chain)
            p.plan[chain[2], "steps"] = chain[0]
        chain[0] += 1


def columns(w, first, rows=0):
    return lambda j: [w[ds(rows + j * SLOT_K * P, SLOT_K * P), ds(first, COLS)]]


def weave(pieces, steps, n, first=2):
    steps = list(steps)
    room = max(n - first - 1, 1)
    given = 0
    for k, _ in enumerate(pieces):
        while given < len(steps) and k >= first + given * room // len(steps):
            steps[given]()
            given += 1
    for step in steps[given:]:
        step()


def norm_scale(p, lane_tokens, x, eps):
    pe, act, dve, pool = p.lanes
    ss = p.ss
    for t in range(NT):
        sq = act.done(on(act, *lane_tokens).activation(p.junk[:, :], x[:, t, :], ACT.Square,
                                                       accum_out=ss[:, t:t + 1]))
    mean = pool.done(on(pool, sq).tensor_scalar(ss[:, 2:4], ss[:, 0:2], 1.0 / D, eps, ALU.mult, ALU.add))
    return pool.done(on(pool, mean).tensor_tensor(p.rstd[:, 0:2], ss[:, 2:4], p.minus_half[:, 0:2], ALU.pow))


def to_operand(p, x, diag_of, gain, operand, after=(), free=()):
    pe, act, dve, pool = p.lanes
    head, rest = operand
    banks = p.ps[2:8]
    read = [None] * len(banks)
    for pair in range(KT // 2):
        n = pair % len(banks)
        bank = banks[n]
        for c in range(2):
            for t in range(NT):
                ct = 2 * pair + c
                m = on(pe, *(after if pair == 0 else ()), read[n] if c + t == 0 else None).matmul(
                    bank[:, c * T + t * P:c * T + (t + 1) * P], x[:, t, ct * P:(ct + 1) * P], diag_of(t),
                    start=True, stop=True)
        turned = pe.done(m)
        for c in range(2):
            ct, src = 2 * pair + c, bank[:, c * T:(c + 1) * T]
            scale = 1.0 if gain is None else gain(ct)
            a = act.done(on(act, turned, *(free if pair + c == 0 else ())).activation(
                head[:, ct, :], src, ACT.Copy, scale=scale))
        for c in range(2):
            ct, src = 2 * pair + c, bank[:, c * T:(c + 1) * T]
            out, h = rest[:, ct, :], head[:, ct, :].bitcast(F32)
            eng = on(dve, a, *(free if pair + c == 0 else ()))
            if gain is None:
                d = dve.done(eng.tensor_tensor(out, src, h, ALU.subtract))
            else:
                d = dve.done(eng.scalar_tensor_tensor(out=out, in0=src, scalar=gain(ct), in1=h, op0=ALU.mult,
                                                      op1=ALU.subtract))
        read[n] = d
    return d


def norm_to_operand(p, x, eps, gain, operand, after=(), free=()):
    pe, act, dve, pool = p.lanes
    scaled = norm_scale(p, after, x, eps)
    for t in range(NT):
        d = dve.done(on(dve, scaled, pe.now()).tensor_scalar(p.diag[:, t, :], p.c("ident"), p.rstd[:, t:t + 1],
                                                             None, ALU.mult))
    return to_operand(p, x, lambda t: p.diag[:, t, :], gain, operand, after=(d, *after), free=free)


PAR = {}
for _name, _n in (("norm_mix", 16), ("norm_xattn", 16), ("norm_mem", 16), ("norm_mlp", 16), ("rwkv_w0", 8),
                  ("rwkv_a0", 8), ("rwkv_k_k", 8), ("rwkv_k_a", 8), ("rwkv_r_k", 8), ("rwkv_ln_w", 8),
                  ("rwkv_ln_b", 8), ("gdn_norm_w", 1), ("mu_lora", 3)):
    PAR[_name] = sum(n for _, n in PAR.values()), _n
PAR["conv"] = 128, 96
PAR["mu"] = 224, 24


def build_program(nc, t, out, plan):
    with ExitStack() as ctx:
        p = Program(nc, ctx, plan)
        pe, act, dve, pool = p.lanes
        sp = p.sp
        p.ps = [ctx.enter_context(nc.psum_tensor(f"bank{i}", [P, 512], F32)) for i in range(8)]
        s = Stream(p)
        operand = p.sb("operand_head", [P, KT, T], F32R), p.sb("operand_rest", [P, KT, T], F32R)
        cst = p.sb("constants", [P, N_CONST])
        par = p.sb("parameters", [P, 2 * P])
        p.junk = p.sb("junk", [P, D], BF16)
        p.ss, p.rstd = p.sb("square_sums", [P, 4]), p.sb("rstd", [P, 4])
        p.minus_half = p.sb("minus_half", [P, 16])
        p.diag = p.sb("diagonals", [P, NT, P])
        a_dt = p.sb("a_log_dt_bias", [P, 2, GDN_H])
        p.c = lambda name: cst[:, CONST[name][0]:CONST[name][0] + CONST[name][1]]

        def pcol(name, k=0):
            at = PAR[name][0] + k
            return par[:, at:at + 1]

        y_store = nc.dram_tensor("y_store", (4 * GDN_H, P, T), F32, kind="Internal").ap()
        t5_store = nc.dram_tensor("t5_store", (AH, P, 2 * T), F32, kind="Internal").ap()
        na_store = nc.dram_tensor("na_store", (AH, GRID, NA_ROW), F32, kind="Internal").ap()
        w = {n: t[n][0] for n in ("w_in", "w_out", "xattn_wq", "xattn_wk", "xattn_wv", "xattn_wo", "mlp_w_up",
                                  "mlp_w_down", "w_in_2", "w_out_2")}
        load_x, load_c, load_p = p.dma_sem("x_arrived"), p.dma_sem("constants_arrived"), p.dma_sem("rows_arrived")

        mix_ctx = ctx.enter_context(ExitStack())
        lora = p.sb("lora", [P, 3, T], ctx=mix_ctx)
        rbuf = p.sb("rwkv_rkv", [P, 24, T], ctx=mix_ctx)
        x_ctx = mix_ctx.enter_context(ExitStack())

        x_nat = p.sb("x", [P, NT, D], ctx=x_ctx)
        x_tok = t["x"][0].rearrange("(t p) d -> p t d", p=P)
        x_in = p.dma(sp, load_x, x_nat[:, :, :], x_tok)
        c_in = p.dma(sp, load_c, cst[:, :], t["consts"])
        rows = p.sb("parameter_rows", [P, 2, P], ctx=x_ctx)
        zeroed = pool.done(pool.engine.memset(rows[:, :, :], 0.0))
        halves = pool.done(pool.engine.memset(p.minus_half[:, :], -0.5))
        wait(sp, zeroed)
        for name, (at, n) in PAR.items():
            a, r = divmod(at, P)
            if name == "mu_lora":
                src = t["rwkv_mu"][0, 3 * RW_W:]
                p.dma(sp, load_p, rows[r:r + 2, a, :], src[0:256].rearrange("(n c) -> n c", c=P))
                p.dma(sp, load_p, rows[r + 2:r + 3, a, 0:32], src[256:288].rearrange("(n c) -> n c", n=1))
                continue
            if name == "conv":
                src = t["gdn_conv_w"][0].rearrange("k (n c) -> (k n) c", c=P)
            elif name == "mu":
                src = t["rwkv_mu"][0, 0:3 * RW_W].rearrange("(n c) -> n c", c=P)
            elif name == "rwkv_r_k":
                src = t[name][0].rearrange("(n a) c -> n (a c)", a=2)
            else:
                src = t[name][0].rearrange("(n c) -> n c", c=P)
            rows_in = p.dma(sp, load_p, rows[r:r + n, a, :], src)
        p.dma(sp, load_p, a_dt[:, 0, :], t["gdn_A_log"][0].partition_broadcast(P))
        rows_in = p.dma(sp, load_p, a_dt[:, 1, :], t["gdn_dt_bias"][0].partition_broadcast(P))

        for a in range(2):
            turned = pe.done(on(pe, rows_in, c_in).transpose(p.ps[2][:, a * P:(a + 1) * P], rows[:, a, :],
                                                             p.c("ident")))
        par_in = dve.done(on(dve, turned).tensor_copy(par[:, :], p.ps[2][:, 0:2 * P]))
        wait(dve, c_in)
        wait(pe, par_in)
        wait(act, par_in)
        wait(pool, halves)
        x_ready = norm_to_operand(p, x_nat, NORM_EPS, lambda ct: pcol("norm_mix", ct), operand, after=(x_in,))

        def narrow(j):
            r = slice(j * SLOT_K * P, (j + 1) * SLOT_K * P)
            return [w["w_in"][r, LORA_COL:LORA_COL + LORA], w["w_in"][r, 4 * GDN_W:4 * GDN_W + 96]]

        s.start(3 * P)

        def read_lora(g, done):
            n = 2 if g == 0 else 1
            return on(act, done).activation(lora[:, 2 * g:2 * g + n, :].rearrange("p a b -> p (a b)"),
                                            s.banks[g][:, 0:n * T], ACT.Copy)

        run(s.block(narrow, operand, True, read_lora, cols=3 * P, ready=(x_ready,)))

        x_ctx.close()
        conv_ctx = mix_ctx.enter_context(ExitStack())
        before = [p.sb(f"before_silu{g}", [P, 2, T], ctx=conv_ctx) for g in range(2)]
        filt = p.sb("filtered", [P, T], ctx=conv_ctx)
        half_tanh = p.sb("half_tanh", [P, T], ctx=conv_ctx)
        y_out = [p.sb(f"silu_out{c}", [P, T], ctx=conv_ctx) for c in range(4)]
        y_sem = [p.dma_sem(f"silu_stored{c}") for c in range(4)]
        filt_w = p.sb("filter_taps", [P, 4, 4], ctx=conv_ctx)
        filt_rows = par[:, 128:224].rearrange("p (k c) -> p k c", k=4)

        def split_T(x, first, after, free):
            for k in range(0, x.shape[1], 4):
                to = slice(first + k, first + k + 4)
                a = act.done(on(act, *after, *free).activation(operand[0][:, to, :], x[:, k:k + 4, :], ACT.Copy))
                d = dve.done(on(dve, a).tensor_tensor(operand[1][:, to, :], x[:, k:k + 4, :],
                                                      operand[0][:, to, :].bitcast(F32), ALU.subtract))
            return d

        t5, dil = p.sb("t5_bias", [32, AH], ctx=conv_ctx), p.sb("dilated", [32, 4 * T], ctx=conv_ctx)
        t5_tab = p.sb("t5_table", [AH, 2 * T], ctx=conv_ctx)
        rpb, na_tab = p.sb("rpb", [AH, 7, 31], ctx=conv_ctx), p.sb("na_table", [AH, 7, P], ctx=conv_ctx)
        load_t, tab_stored = p.dma_sem("tables_arrived"), p.dma_sem("tables_stored")
        p.dma(act, load_t, t5[:, :], t["t5_bias_2"])
        p.dma(act, load_t, dil[:, :], t["dilated"])
        tab_in = p.dma(act, load_t, rpb[:, :, :], t["na_rpb_2"][0, :, 4:11, :])
        m = pe.done(on(pe, tab_in).matmul(p.ps[7][0:AH, :], t5[:, :], dil[:, 0:2 * T], start=True, stop=True))
        dve.done(on(dve, tab_in).memset(na_tab[:, :, :], 0.0))
        dve.done(on(dve).tensor_scalar(na_tab[:, :, 48:79], rpb[:, :, :], 8.0, None, ALU.mult))
        d = dve.done(on(dve, m).scalar_tensor_tensor(out=t5_tab[:, :], in0=p.ps[7][0:AH, :], scalar=8.0,
                                                     in1=dil[0:AH, 2 * T:4 * T], op0=ALU.mult, op1=ALU.add))
        wait(act, d)
        p.dma(act, tab_stored, t5_store, bc(t5_tab[:, :].unsqueeze(1), AH, P, 2 * T))
        p.dma(act, tab_stored, na_store, bc(na_tab[:, :, :].rearrange("h r j -> h (r j)").unsqueeze(1), AH, GRID, NA_ROW))

        def keep_raw(g, done):
            return on(act, done, dve.now()).activation(before[g][:, :, :].rearrange("p a b -> p (a b)"),
                                                       s.banks[g][:, :], ACT.Copy)

        def silu_steps(first, conv):
            left = s.block_no.at

            tok = {}

            def source(c):
                return filt[:, :] if conv else before[c // 2][:, c % 2, :]

            def filtered(c):
                def step():
                    raw = before[c // 2][:, c % 2, :]
                    tok["x"] = (s.evacuated[c // 2], left)
                    if not conv:
                        return
                    if c == 0:
                        dve.done(on(dve).tensor_copy(filt_w[:, :, :], filt_rows[:, :, ds(first, 4)]))
                    d = dve.done(on(dve, tok["x"], act.now()).tensor_scalar(filt[:, :], raw, filt_w[:, 3, c:c + 1], None, ALU.mult))
                    for shift in range(1, 4):
                        o = filt[:, shift:T]
                        d = dve.done(on(dve, d).scalar_tensor_tensor(
                            out=o, in0=raw[:, 0:T - shift], scalar=filt_w[:, 3 - shift, c:c + 1], in1=o,
                            op0=ALU.mult, op1=ALU.add))
                    tok["x"] = d
                return step

            def tanh(c):
                def step():
                    tok["t"] = act.done(on(act, tok["x"], dve.now()).activation(half_tanh[:, :], source(c), ACT.Tanh, scale=0.5))
                return step

            def times(c):
                def step():
                    wait(dve, y_sem[c].now())
                    tok["y", c] = dve.done(on(dve, tok["t"], tok["x"]).scalar_tensor_tensor(
                        out=y_out[c][:, :], in0=half_tanh[:, :], scalar=1.0, in1=source(c), op0=ALU.add, op1=ALU.mult))
                return step

            def store(c):
                def step():
                    wait(act, tok["y", c])
                    p.dma(act, y_sem[c], y_store[ds(first + c, 1), :, :].rearrange("a p t -> (a p) t"), y_out[c][:, :])
                return step

            steps = []
            for c in range(4):
                steps += [filtered(c), tanh(c)] + ([store(c - 1)] if c else []) + [times(c)]
            return steps + [store(3)]

        w_in = w["w_in"]
        for c in range(4):
            dve.engine.memset(y_out[c][:, :], 0.0).then_inc(y_sem[c].sem, 16)
            y_sem[c].at = y_sem[c].at + 16
        run(s.block(columns(w_in, 0), operand, True, keep_raw))
        with p.loop("qkv", 5) as loop:
            steps = silu_steps(loop.i * 4, True)
            weave(s.block(columns(w_in, (loop.i + 1) * COLS), operand, True, keep_raw), steps, 32)
        weave(s.block(columns(w_in, 6 * COLS), operand, True, keep_raw), silu_steps(20, True), 32)
        weave(s.block(columns(w_in, 7 * COLS), operand, True, keep_raw), silu_steps(24, False), 32)


        def keep_rwkv(first):
            def read(g, done):
                return on(act, done).activation(rbuf[:, ds(first + 2 * g, 2), :].rearrange("p a b -> p (a b)"),
                                                s.banks[g][:, :], ACT.Copy)
            return read

        weave(s.block(columns(w_in, GDN_COLS), operand, True, keep_rwkv(0)), silu_steps(28, False), 32)
        with p.loop("rwkv_columns", 5) as loop:
            run(s.block(columns(w_in, (loop.i + 1) * COLS + GDN_COLS), operand, True, keep_rwkv(loop.i * 4 + 4)))
        wait(act, *[c.now() for c in y_sem])
        wait(act, tab_stored.now())
        conv_ctx.close()
        gdn_ctx = mix_ctx.enter_context(ExitStack())

        ident, ones = p.c("ident"), p.c("ones")
        bank = p.ps[2]
        scal = p.sb("gdn_scalars", [P, GDN_H, 9], ctx=gdn_ctx)
        G_0, BETA_0, HALF_BETA_0, TAIL, DECAY, MINUS_DECAY = 0, 2, 4, 6, 7, 8
        gate = p.sb("gates", [P, 6, NT, GDN_H], ctx=gdn_ctx)
        x, ax, sp_, g, tb, _ = (gate[:, i, :, :] for i in range(6))
        ea = p.sb("exp_a_log", [P, GDN_H], ctx=gdn_ctx)
        p.join()
        for i in range(NT):
            m = pe.engine.transpose(bank[:, i * P:(i + 1) * P], lora[:, 2, i * P:(i + 1) * P], ident)
        turned = pe.done(m)
        ab = bank[:, 0:NT * P].rearrange("p (t c) -> p t c", t=NT)

        def over_tiles(v):
            return bc(v.unsqueeze(1), P, NT, GDN_H)

        dve.done(on(dve, turned).tensor_tensor(x, ab[:, :, 32:40], over_tiles(a_dt[:, 1, :]), ALU.add))
        moved = dve.done(on(dve).tensor_scalar(tb, ab[:, :, 40:48], 0.5, None, ALU.mult))
        dve.done(on(dve).tensor_scalar(ax, x, -1.0, None, ALU.mult))
        d = dve.done(on(dve).tensor_tensor(ax, ax, x, ALU.max))
        act.done(on(act, d).activation(tb, tb, ACT.Tanh))
        act.done(on(act).activation(ea[:, :], a_dt[:, 0, :], ACT.Exp))
        act.done(on(act).activation(ax, ax, ACT.Exp, scale=-1.0))
        a = act.done(on(act).activation(sp_, ax, ACT.Ln, bias=1.0))
        dve.done(on(dve, a).scalar_tensor_tensor(out=sp_, in0=x, scalar=0.0, in1=sp_, op0=ALU.max, op1=ALU.add))
        g_made = dve.done(on(dve).scalar_tensor_tensor(out=g, in0=sp_, scalar=-1.0, in1=over_tiles(ea[:, :]),
                                                       op0=ALU.mult, op1=ALU.mult))
        for i in range(NT):
            put = lambda k, src, *a: dve.done(on(dve).tensor_scalar(scal[:, :, k + i], src, *a))
            dve.done(on(dve).tensor_copy(scal[:, :, G_0 + i], g[:, i, :]))
            put(BETA_0, tb[:, i, :], 0.5, 0.5, ALU.mult, ALU.add)
            put(HALF_BETA_0, tb[:, i, :], 0.25, 0.25, ALU.mult, ALU.add)
        pe_sum = on(pe, g_made, moved)
        pe_sum.matmul(bank[:, 0:8], p.c("le"), g[:, 1, :], start=True, stop=True)
        summed = pe.done(pe_sum.matmul(bank[:, 8:16], p.c("gt"), g[:, 0, :], start=True, stop=True))
        act.done(on(act, summed, dve.now()).activation(scal[:, :, DECAY], bank[:, 0:8], ACT.Exp))
        a = act.done(on(act).activation(scal[:, :, TAIL], bank[:, 8:16], ACT.Exp))
        scalars = dve.done(on(dve, a).tensor_scalar(scal[:, :, MINUS_DECAY], scal[:, :, DECAY], -1.0, None, ALU.mult))
        half_norm = p.sb("half_gdn_norm", [P, 1], ctx=gdn_ctx)
        eps_col = p.sb("gdn_norm_rows", [P, 2, 4], ctx=gdn_ctx)
        dve.done(on(dve).tensor_scalar(half_norm[:, :], pcol("gdn_norm_w"), 0.5, None, ALU.mult))
        dve.done(on(dve).memset(eps_col[:, 0, 0:2], 1.0))
        dve.done(on(dve).memset(eps_col[:, 0, 2:4], GDN_D ** -0.5))

        def gdn_tile(name, *shape):
            return p.sb("gdn_" + name, [P, *shape], ctx=gdn_ctx)

        level = p.c("level").rearrange("p (l i) -> p l i", l=7)

        def gdn_heads():
            hs, qkvz = gdn_tile("head_scalars", 9), gdn_tile("head_qkvz", 4, T)
            load_y = p.dma_sem("head_qkvz_arrived")
            lv = gdn_tile("gamma_or_m_level", 2, NT, P)
            le_g, gamma = lv[:, 0, :, :], lv[:, 1, :, :]
            gm = gdn_tile("gamma_masked", NT, 2, P)
            ss, rs = gdn_tile("square_sums", 4), gdn_tile("inverse_norms", 4)
            kq, kb, vb = gdn_tile("kq", 4, P), gdn_tile("k_beta", NT, P), gdn_tile("v_beta", NT, P)
            k_tail, k_T, bq_T = gdn_tile("k_tail", P), gdn_tile("k_T", NT, P), gdn_tile("k_beta_q_T", NT, 2, P)
            ma = gdn_tile("m_a_T", NT, 2, P)
            xq, yy = gdn_tile("inverse", 2, NT, P), gdn_tile("level_product", NT, P)
            st, rr, qs = gdn_tile("state", P), gdn_tile("rhs", P), gdn_tile("q_state", P)
            u, o = kb, k_T
            sq = gdn_tile("squares", P)
            y4 = y_store.rearrange("(k h) p t -> k h p t", k=4)

            def two(bank, n=2):
                return bank[:, 0:n * P].rearrange("p (a c) -> p a c", a=n)

            def gdn_head(h):
                b0 = b4 = p.ps[2]
                b1 = b3 = p.ps[3]
                b2 = b5 = p.ps[4]
                ready = p.dma(act, load_y, qkvz[:, :, :], y4[:, ds(h, 1), :, :].rearrange("k h p t -> (h p) k t"))
                staged = dve.done(on(dve).tensor_copy(hs[:, :], scal[:, ds(h, 1), :].rearrange("p a k -> p (a k)")))
                yield
                for i in range(NT):
                    a = act.done(on(act, staged).activation(le_g[:, i, :], p.c("le"), ACT.Copy, scale=hs[:, G_0 + i:G_0 + i + 1]))
                    yield
                for i in range(NT):
                    m = on(pe, a, *turn_start[1:]).matmul(b5[:, i * P:(i + 1) * P], p.c("gt"), le_g[:, i, :], start=True, stop=True)
                summed = pe.done(m)
                yield
                for n in range(4):
                    m = on(pe, ready, *turn_start[1:]).transpose(b0[:, n * P:(n + 1) * P], qkvz[:, 1 - n // 2, (n % 2) * P:(n % 2 + 1) * P], ident)
                kq_turned = pe.done(m)
                yield
                for n in range(2):
                    m = pe.engine.transpose(b1[:, n * P:(n + 1) * P], qkvz[:, 2, n * P:(n + 1) * P], ident)
                v_turned = pe.done(m)
                yield
                e = act.done(on(act, summed).activation(gamma[:, :, :], two(b5), ACT.Exp))
                yield
                gm_made = pool.done(on(pool, e).tensor_tensor(
                    gm[:, :, :, :], bc(gamma[:, :, :].unsqueeze(2), P, NT, 2, P),
                    bc(p.c("gdn_mask").rearrange("p (k c) -> p k c", k=2).unsqueeze(1), P, NT, 2, P), ALU.mult))
                yield
                for n in range(4):
                    a = act.done(on(act, kq_turned).activation(sq[:, :], b0[:, n * P:(n + 1) * P], ACT.Square,
                                                               accum_out=ss[:, n:n + 1]))
                    yield
                d = dve.done(on(dve, a).tensor_scalar(ss[:, :], ss[:, :], 4e-6, None, ALU.add))
                yield
                pool.done(on(pool, d).tensor_tensor(rs[:, :], ss[:, :], p.minus_half[:, 0:4], ALU.pow))
                yield
                r = pool.done(on(pool).tensor_tensor(rs[:, :], rs[:, :], eps_col[:, 0, :], ALU.mult))
                yield
                vb_made = dve.done(on(dve, v_turned).tensor_tensor(
                    vb[:, :, :], two(b1), bc(hs[:, HALF_BETA_0:HALF_BETA_0 + 2].unsqueeze(2), P, NT, P), ALU.mult))
                yield
                kq_made = dve.done(on(dve, r).tensor_tensor(kq[:, :, :], two(b0, 4), bc(rs[:, :].unsqueeze(2), P, 4, P), ALU.mult))
                yield
                kb_made = dve.done(on(dve).tensor_tensor(
                    kb[:, :, :], kq[:, 0:2, :], bc(hs[:, BETA_0:BETA_0 + 2].unsqueeze(2), P, NT, P), ALU.mult))
                yield
                tail = act.done(on(act, kq_made).activation(k_tail[:, :], kq[:, 0, :], ACT.Copy, scale=hs[:, TAIL:TAIL + 1]))
                yield
                for n in range(4):
                    m = on(pe, kq_made, e).transpose(b2[:, n * P:(n + 1) * P], kq[:, n, :], ident)
                kq_back = pe.done(m)
                yield
                for n in range(2):
                    m = on(pe, kb_made).transpose(b3[:, n * P:(n + 1) * P], kb[:, n, :], ident)
                kb_back = pe.done(m)
                yield
                act.done(on(act, kq_back).activation(k_T[:, :, :], two(b2), ACT.Copy))
                yield
                act.done(on(act).activation(bq_T[:, :, 1, :], b2[:, 2 * P:4 * P].rearrange("p (a c) -> p a c", a=2), ACT.Copy))
                yield
                a = act.done(on(act, kb_back).activation(bq_T[:, :, 0, :], two(b3), ACT.Copy))
                yield
                for i in range(NT):
                    m = on(pe, a).matmul(b4[:, i * 2 * P:(i + 1) * 2 * P], k_T[:, i, :],
                                         bq_T[:, i, :, :].rearrange("p a c -> p (a c)"), start=True, stop=True)
                gram = pe.done(m)
                yield
                ma_made = dve.done(on(dve, gram, gm_made).tensor_tensor(
                    ma[:, :, :, :].rearrange("p a k c -> p (a k c)"), b4[:, :], gm[:, :, :, :].rearrange("p a k c -> p (a k c)"),
                    ALU.mult))
                yield
                m_T = ma[:, :, 0, :]

                def at_level(l):
                    return bc(level[:, l, :].unsqueeze(1), P, NT, P)

                lv_made = pool.done(on(pool, ma_made).tensor_tensor(lv[:, 1, :, :], m_T, at_level(1), ALU.mult))
                yield
                dve.done(on(dve).tensor_tensor(lv[:, 0, :, :], m_T, at_level(0), ALU.mult))
                yield
                q_made = dve.done(on(dve).tensor_tensor(xq[:, 1, :, :], bc(ident.unsqueeze(1), P, NT, P), lv[:, 0, :, :], ALU.subtract))
                yield
                for i in range(NT):
                    m = on(pe, q_made).transpose(b0[:, i * P:(i + 1) * P], xq[:, 1, i, :], ident)
                x_made = act.done(on(act, pe.done(m)).activation(xq[:, 0, :, :], two(b0), ACT.Copy))
                yield
                for l in range(1, 7):
                    for i in range(NT):
                        m = on(pe, lv_made, x_made, q_made).matmul(b1[:, i * P:(i + 1) * P], lv[:, l % 2, i, :], xq[:, 0, i, :],
                                                           start=True, stop=True)
                    y_done = pe.done(m)
                    yield
                    if l < 6:
                        lv_made = pool.done(on(pool, y_done, q_made).tensor_tensor(lv[:, (l + 1) % 2, :, :], m_T, at_level(l + 1), ALU.mult))
                        yield
                    y_made = act.done(on(act, y_done).activation(yy[:, :, :], two(b1), ACT.Copy))
                    yield
                    lo = 1 if l == 6 else 0
                    for i in range(NT):
                        if not lo:
                            on(pe, y_made).matmul(b2[:, i * P:(i + 1) * P], xq[:, 1, i, :], yy[:, i, :], start=True, stop=True)
                        m = on(pe, y_made).matmul(b2[:, (2 + i) * P:(3 + i) * P], yy[:, i, :], xq[:, 1, i, :], start=True, stop=True)
                    z_done = pe.done(m)
                    yield
                    q_made = x_made = dve.done(on(dve, z_done).tensor_tensor(
                        xq[:, lo:2, :, :].rearrange("p a b c -> p (a b c)"), xq[:, lo:2, :, :].rearrange("p a b c -> p (a b c)"),
                        b2[:, lo * 2 * P:4 * P], ALU.subtract))
                    yield
                m = pe.done(on(pe, q_made, vb_made).matmul(b3[:, 0:P], xq[:, 1, 0, :], vb[:, 0, :], start=True, stop=True))
                yield
                u0 = act.done(on(act, m).activation(u[:, 0, :], b3[:, 0:P], ACT.Copy))
                yield
                m = pe.done(on(pe, u0, tail).matmul(b4[:, 0:P], k_tail[:, :], u[:, 0, :], start=True, stop=True))
                yield
                pe.engine.matmul(b5[:, 0:P], ma[:, 0, 1, :], u[:, 0, :], start=True, stop=True)
                s_made = act.done(on(act, m).activation(st[:, :], b4[:, 0:P], ACT.Copy))
                yield
                m = pe.done(on(pe, s_made).matmul(b3[:, 0:P], bq_T[:, 1, 0, :], st[:, :], start=True, stop=True))
                yield
                m2 = pe.done(pe.engine.matmul(b4[:, 0:P], bq_T[:, 1, 1, :], st[:, :], start=True, stop=True))
                yield
                r_made = dve.done(on(dve, m).scalar_tensor_tensor(out=rr[:, :], in0=b3[:, 0:P], scalar=hs[:, MINUS_DECAY:MINUS_DECAY + 1],
                                                                  in1=vb[:, 1, :], op0=ALU.mult, op1=ALU.add))
                yield
                qs_made = act.done(on(act, m2).activation(qs[:, :], b4[:, 0:P], ACT.Copy, scale=hs[:, DECAY:DECAY + 1]))
                yield
                m = pe.done(on(pe, r_made).matmul(b3[:, 0:P], xq[:, 1, 1, :], rr[:, :], start=True, stop=True))
                yield
                u1 = act.done(on(act, m).activation(u[:, 1, :], b3[:, 0:P], ACT.Copy))
                yield
                m = pe.done(on(pe, u1).matmul(b5[:, P:2 * P], ma[:, 1, 1, :], u[:, 1, :], start=True, stop=True))
                yield
                dve.done(on(dve, m).tensor_copy(o[:, 0, :], b5[:, 0:P]))
                yield
                o_made = dve.done(on(dve, qs_made).tensor_tensor(o[:, 1, :], b5[:, P:2 * P], qs[:, :], ALU.add))
                yield
                for i in range(NT):
                    a = act.done(on(act, o_made).activation(sq[:, :], o[:, i, :], ACT.Square, accum_out=ss[:, i:i + 1]))
                    yield
                d = dve.done(on(dve, a).tensor_scalar(ss[:, 0:2], ss[:, 0:2], 1.0 / GDN_D, NORM_EPS, ALU.mult, ALU.add))
                yield
                r = pool.done(on(pool, d).tensor_tensor(rs[:, 0:2], ss[:, 0:2], p.minus_half[:, 0:2], ALU.pow))
                yield
                d = dve.done(on(dve, r).tensor_tensor(o[:, :, :], o[:, :, :], bc(rs[:, 0:2].unsqueeze(2), P, NT, P), ALU.mult))
                yield
                for i in range(NT):
                    m = on(pe, d).transpose(b0[:, i * P:(i + 1) * P], o[:, i, :], ident)
                m = pe.done(m)
                yield
                dve.done(on(dve, m).scalar_tensor_tensor(
                    out=mixg[:, ds(h, 1), :].rearrange("p a t -> p (a t)"), in0=b0[:, 0:T], scalar=half_norm[:, 0:1],
                    in1=qkvz[:, 3, :], op0=ALU.mult, op1=ALU.mult))
                yield
            return gdn_head

        gdn_head = gdn_heads()

        turn_start = []
        k_store = nc.dram_tensor("k_store", (KT, P, T), F32, kind="Internal").ap()
        v_store = nc.dram_tensor("v_store", (P, NT, D), F32, kind="Internal").ap()
        load_m = p.dma_sem("mem_arrived")
        rw_ctx = gdn_ctx.enter_context(ExitStack())

        def rw_tile(name, *shape):
            return p.sb("rw_" + name, [P, *shape], ctx=rw_ctx)

        rp = rw_tile("pair_columns", RW_PAIRS, 14)
        (HALF_W0, HALF_A0, K_K, K_A, ONE_K_A, R_K, LN_W, LN_B) = range(8)
        MU, ONE_MU = 8, 11
        w_small, w_gate, w_gate2 = rw_tile("w2_a2", P), rw_tile("g2", P), rw_tile("g2_end", P)
        lo = rw_tile("lora_shifted", 3, T)
        one_mu = rw_tile("one_minus_mu", 4)
        mixg = rbuf[:, 8:16, :]
        mem_ctx = rw_ctx.enter_context(ExitStack())
        mem_nat = p.sb("mem", [P, NT, D], ctx=mem_ctx)
        p.join(act)
        mem_in = p.dma(act, load_m, mem_nat[:, :, :], t["mem"][0].rearrange("(t p) d -> p t d", p=P))
        p.join()

        def pair_cols(name, n=8, at=0):
            a = PAR[name][0] + at
            return par[:, a:a + n]

        def setp(k, src, a=1.0, b=0.0):
            return dve.done(on(dve).tensor_scalar(rp[:, :, k], src, a, b, ALU.mult, ALU.add))

        setp(HALF_W0, pair_cols("rwkv_w0"), 0.5)
        setp(HALF_A0, pair_cols("rwkv_a0"), 0.5)
        setp(K_K, pair_cols("rwkv_k_k"))
        setp(K_A, pair_cols("rwkv_k_a"))
        setp(ONE_K_A, pair_cols("rwkv_k_a"), -1.0, 1.0)
        setp(R_K, pair_cols("rwkv_r_k"))
        setp(LN_W, pair_cols("rwkv_ln_w"))
        setp(LN_B, pair_cols("rwkv_ln_b"))
        for k in range(3):
            setp(MU + k, pair_cols("mu", 8, 8 * k))
            setp(ONE_MU + k, pair_cols("mu", 8, 8 * k), -1.0, 1.0)
        mu_l = par[:, PAR["mu_lora"][0]:PAR["mu_lora"][0] + 3]
        dve.done(on(dve).tensor_scalar(one_mu[:, 0:3], mu_l, -1.0, 1.0, ALU.mult, ALU.add))

        def shifted(out, y, mu, keep):
            dve.done(on(dve).tensor_scalar(out, y, keep, None, ALU.mult))
            return dve.done(on(dve).scalar_tensor_tensor(out=out[:, 1:T], in0=y[:, 0:T - 1], scalar=mu,
                                                         in1=out[:, 1:T], op0=ALU.mult, op1=ALU.add))

        for k in range(3):
            d = shifted(lo[:, k, :], lora[:, k, :], mu_l[:, k:k + 1], one_mu[:, k:k + 1])
        act.done(on(act, d).activation(lo[0:64, 0, :], lo[0:64, 0, :], ACT.Tanh))
        for part in (lo[:, 1, :], lo[0:32, 2, :]):
            a = act.done(on(act).activation(part, part, ACT.Tanh, scale=0.5))
            d = dve.done(on(dve, a).tensor_scalar(part, part, 0.5, 0.5, ALU.mult, ALU.add))
        free = s.last_used()
        mem_ready = norm_to_operand(p, mem_nat, NORM_EPS, lambda ct: pcol("norm_mem", ct), operand,
                                    after=(mem_in,), free=(free,))
        p.join()
        mem_ctx.close()

        pst = rw_tile("columns", 14)
        early = rw_tile("rkv_tanh_or_inverse", 6, T)
        rkv, th_w, th_a, k2 = early[:, 0:3, :], early[:, 3, :], early[:, 4, :], early[:, 5, :]
        xr, qr, yr = (early[:, 2 * k:2 * k + 2, :].rearrange("p a (s c) -> p (a s) c", s=2) for k in range(3))
        decays = rw_tile("decays_or_m_level", 4, T)
        cum, e_in, e_out, e_ex = (decays[:, k, :] for k in range(4))
        lvr = decays[:, :, :].rearrange("p (b a) (s c) -> p b (a s) c", b=2, s=2)
        units = rw_tile("k_unit_or_u", 2, T)
        kk, ka = units[:, 0, :], units[:, 1, :]
        nv, ur = (units[:, k, :].rearrange("p (s c) -> p s c", s=4) for k in range(2))
        orw, osq = (lora[:, k, :].rearrange("p (s c) -> p s c", s=4) for k in range(2))
        xa_T = lora[:, 2, :]
        e_state, gate_T = rw_tile("state_decay", 4), rw_tile("gate", T)
        sqr, bv = rw_tile("k_squares", T), rw_tile("bonus_v", T)
        rs4, ss4 = rw_tile("inverse_norms", 4), rw_tile("square_sums", 4)
        rsb = rw_tile("inverse_norms_wide", NT, P)
        ar, b_T, k_T = rw_tile("a_r_T", NT, 2, P), rw_tile("b_T", T), rw_tile("kd_T", T)
        vb_n, ka_n = rw_tile("v_b_natural", 4, P), rw_tile("k_a_natural", 4, P)
        gr = rw_tile("grams_T", 4, 4, P)
        zs = rw_tile("states", 4, P)
        stat = rw_tile("o_stats", 4, 4)
        kv_out = [rw_tile(f"kv_out{g}", COLS) for g in range(2)]
        small = [p.dma_sem("small_weights_arrived")]
        kv_sem = [p.dma_sem(f"kv_stored{g}") for g in range(2)]
        dve.done(on(dve).memset(zs[:, 0, :], 0.0))
        dve.done(on(dve).memset(w_gate2[:, :], 0.0))
        for g in range(2):
            dve.engine.memset(kv_out[g][:, :], 0.0).then_inc(kv_sem[g].sem, 16)
            kv_sem[g].at = kv_sem[g].at + 16
        DECAY_SCALE = -0.5 * math.exp(-0.5)

        def u_of(rows, i):
            return ur[rows, :, :].rearrange("p (a t) c -> p t a c", a=2)[:, i, :, :]

        def heads2(ap):
            return ap.rearrange("p (a c) -> p a c", a=2)

        def sys4(bank):
            return bank[:, :].rearrange("p (s c) -> p s c", s=4)

        def rwkv_pair(q):
            bx, by, bz = p.ps[5:8]
            for dst, src in ((w_small[0:64, :], t["rwkv_w2"][0, :, ds(q * P, P)]), (w_small[64:128, :], t["rwkv_a2"][0, :, ds(q * P, P)]),
                             (w_gate[:, :], t["rwkv_g2"][0, 0:P, ds(q * P, P)]), (w_gate2[0:32, :], t["rwkv_g2"][0, P:P + 32, ds(q * P, P)])):
                small_in = p.dma(act, small[0], dst, src)
            dve.done(on(dve).tensor_copy(pst[:, :], rp[:, ds(q, 1), :].rearrange("p a k -> p (a k)")))
            yield
            col = lambda k: pst[:, k:k + 1]
            for k in range(3):
                d = shifted(rkv[:, k, :], rbuf[:, ds(q + 8 * k, 1), :].rearrange("p a t -> p (a t)"), col(MU + k), col(ONE_MU + k))
                if k == 1:
                    rk_in = d
            v_in = d
            yield
            r_, k_, v_ = (rkv[:, k, :] for k in range(3))
            pe_in = on(pe, small_in, *turn_start[1:])
            w_done = pe.done(pe_in.matmul(bx[:, 0:T], w_small[0:64, :], lo[0:64, 0, :], start=True, stop=True))
            yield
            a_done = pe.done(pe_in.matmul(by[:, 0:T], w_small[64:128, :], lo[64:128, 0, :], start=True, stop=True))
            yield
            pe_in.matmul(bz[:, 0:T], w_gate[:, :], lo[:, 1, :], start=True, stop=False)
            g_done = pe.done(pe_in.matmul(bz[:, 0:T], w_gate2[:, :], lo[:, 2, :], start=False, stop=True))
            yield
            tw = act.done(on(act, w_done, rk_in).activation(th_w[:, :], bx[:, 0:T], ACT.Tanh, scale=0.5, bias=col(HALF_W0)))
            yield
            ta = act.done(on(act, a_done).activation(th_a[:, :], by[:, 0:T], ACT.Tanh, scale=0.5, bias=col(HALF_A0)))
            yield
            gT = act.done(on(act, g_done).activation(gate_T[:, :], bz[:, 0:T], ACT.Copy))
            yield
            d = dve.done(on(dve).tensor_scalar(kk[:, :], k_, col(K_K), None, ALU.mult))
            yield
            a = act.done(on(act, d).activation(sqr[:, :], kk[:, :], ACT.Square))
            yield
            for i in range(NT):
                m = on(pe, a, tw).matmul(bx[:, 2 * i:2 * i + 2], sqr[:, i * P:(i + 1) * P], p.c("headsel"), start=True, stop=True)
            d = dve.done(on(dve, pe.done(m)).tensor_scalar(ss4[:, :], bx[:, 0:4], 1e-6, None, ALU.add))
            yield
            r4 = pool.done(on(pool, d).tensor_tensor(rs4[:, :], ss4[:, :], p.minus_half[:, 0:4], ALU.pow))
            yield
            dve.done(on(dve, tw).tensor_scalar(th_w[:, :], th_w[:, :], 1.0, DECAY_SCALE, ALU.add, ALU.mult))
            yield
            dve.done(on(dve).tensor_tensor_scan(cum[:, :], p.c("reset"), th_w[:, :], 0.0, ALU.mult, ALU.add))
            yield
            c4 = cum[:, :].rearrange("p (c t) -> p c t", c=4)
            mids = dve.done(on(dve).tensor_copy(stat[:, 0, :], c4[:, :, RW_C // 2 - 1]))
            yield
            dve.done(on(dve).tensor_tensor(c4, c4, bc(stat[:, 0, :].unsqueeze(2), P, 4, RW_C), ALU.subtract))
            yield
            centred = dve.done(on(dve).tensor_tensor(e_ex[:, :], cum[:, :], th_w[:, :], ALU.subtract))
            yield
            ends = dve.done(on(dve).tensor_tensor(e_state[:, 0:3], c4[:, 0:3, RW_C - 1], stat[:, 0, 1:4], ALU.add))
            yield
            act.done(on(act, centred).activation(e_in[:, :], cum[:, :], ACT.Exp))
            yield
            act.done(on(act).activation(e_out[:, :], cum[:, :], ACT.Exp, scale=-1.0))
            yield
            act.done(on(act).activation(e_ex[:, :], e_ex[:, :], ACT.Exp))
            yield
            exps = act.done(on(act, ends).activation(e_state[:, 0:3], e_state[:, 0:3], ACT.Exp))
            yield
            dve.done(on(dve, r4).tensor_copy(rsb[:, :, :].rearrange("p t (h c) -> p (t h) c", h=2), bc(rs4[:, :].unsqueeze(2), P, 4, RW_D)))
            yield
            wide = dve.now()
            dve.done(on(dve, ta).tensor_scalar(th_a[:, :], th_a[:, :], 0.5, 0.5, ALU.mult, ALU.add))
            yield
            dve.done(on(dve).tensor_scalar(k2[:, :], th_a[:, :], col(K_A), col(ONE_K_A), ALU.mult, ALU.add))
            yield
            k2_made = dve.done(on(dve).tensor_tensor(k2[:, :], k2[:, :], k_, ALU.mult))
            yield
            for i in range(NT):
                m = on(pe, wide).matmul(bx[:, i * P:(i + 1) * P], rsb[:, i, :], ident, start=True, stop=True)
            scale_done = pe.done(m)
            yield
            pool.done(on(pool, k2_made, exps).tensor_tensor(k_T[:, :], k2[:, :], e_out[:, :], ALU.mult))
            yield
            ar_v = lambda k: ar[:, :, k, :]
            tt = lambda ap: ap.rearrange("p (t c) -> p t c", t=NT)
            pool.done(on(pool).tensor_tensor(ar_v(1), tt(r_), tt(e_in[:, :]), ALU.mult))
            yield
            rk_made = dve.done(on(dve).scalar_tensor_tensor(out=bv[:, :], in0=r_, scalar=col(R_K), in1=k2[:, :], op0=ALU.mult, op1=ALU.mult))
            yield
            kk_made = dve.done(on(dve, scale_done).tensor_tensor(kk[:, :], kk[:, :], bx[:, 0:T], ALU.mult))
            yield
            dve.done(on(dve, exps).scalar_tensor_tensor(out=ar_v(0), in0=tt(kk[:, :]), scalar=-1.0, in1=tt(e_ex[:, :]), op0=ALU.mult, op1=ALU.mult))
            yield
            dve.done(on(dve).tensor_tensor(ka[:, :], kk[:, :], th_a[:, :], ALU.mult))
            yield
            made = dve.done(on(dve).tensor_tensor(b_T[:, :], ka[:, :], e_out[:, :], ALU.mult))
            yield
            made2 = pool.now()
            m = pe.done(on(pe, rk_made).matmul(by[:, 0:T], p.c("blockones"), bv[:, :], start=True, stop=True))
            yield
            bonus = dve.done(on(dve, m).tensor_tensor(bv[:, :], by[:, 0:T], v_, ALU.mult))
            yield
            wait(pe, made, made2, v_in, gT)
            for n, (x, y) in enumerate(((v_, k_T[:, :]), (b_T[:, :], None))):
                for i in range(NT):
                    pe.engine.transpose(bz[:, (2 * n + i) * P:(2 * n + i + 1) * P], x[:, i * P:(i + 1) * P], ident)
                    src = y[:, i * P:(i + 1) * P] if y is not None else ar[:, i, 0, :]
                    m = pe.engine.transpose(bx[:, (2 * n + i) * P:(2 * n + i + 1) * P], src, ident)
            turned = pe.done(m)
            yield
            vb_made = act.done(on(act, turned).activation(vb_n[:, :, :], sys4(bz), ACT.Copy))
            yield
            nat_made = act.done(on(act).activation(ka_n[:, :, :], sys4(bx), ACT.Copy))
            yield
            free = bonus, vb_made, nat_made, None
            for n in range(4):
                a, i = divmod(n, 2)
                c, bank = slice(RW_D * a, RW_D * (a + 1)), (by, bz, bx, by)[n]
                rhs = ar[c, i, :, :].rearrange("p k t -> p (k t)")
                wait(pe, free[n] if n < 3 else grams)
                pe.engine.matmul(bank[:, 0:2 * P], b_T[c, i * P:(i + 1) * P], rhs, start=True, stop=True)
                m = pe.engine.matmul(bank[:, 2 * P:4 * P], k_T[c, i * P:(i + 1) * P], rhs, start=True, stop=True)
                d = dve.done(on(dve, pe.done(m)).tensor_tensor(gr[:, n, :, :], sys4(bank),
                                                               p.c("rw_mask").rearrange("p (k c) -> p k c", k=4), ALU.mult))
                yield
                grams = d
            n_T = gr[:, :, 0, :]

            def at_level(l):
                return bc(level[:, l, :].unsqueeze(1), P, 4, P)

            l_made = pool.done(on(pool, grams).tensor_tensor(lvr[:, 1, :, :], n_T, at_level(1), ALU.mult))
            yield
            dve.done(on(dve).tensor_tensor(qr[:, :, :], n_T, at_level(0), ALU.mult))
            yield
            q_made = dve.done(on(dve).tensor_tensor(qr[:, :, :], qr[:, :, :], bc(ident.unsqueeze(1), P, 4, P), ALU.add))
            yield
            for n in range(4):
                m = on(pe, q_made).transpose(bz[:, n * P:(n + 1) * P], qr[:, n, :], ident)
            x_made = act.done(on(act, pe.done(m)).activation(xr[:, :, :], sys4(bz), ACT.Copy))
            yield
            for l in range(1, 6):
                for n in range(4):
                    m = on(pe, l_made, x_made, q_made).matmul(bx[:, n * P:(n + 1) * P], lvr[:, l % 2, n, :], xr[:, n, :], start=True, stop=True)
                y_done = pe.done(m)
                yield
                if l < 5:
                    l_made = pool.done(on(pool, y_done).tensor_tensor(lvr[:, (l + 1) % 2, :, :], n_T, at_level(l + 1), ALU.mult))
                    yield
                y_made = act.done(on(act, y_done).activation(yr[:, :, :], sys4(bx), ACT.Copy))
                yield
                if l < 5:
                    for n in range(4):
                        m = on(pe, y_made).matmul(by[:, n * P:(n + 1) * P], qr[:, n, :], yr[:, n, :], start=True, stop=True)
                    z_done = pe.done(m)
                    yield
                for n in range(4):
                    m = on(pe, y_made).matmul(bz[:, n * P:(n + 1) * P], yr[:, n, :], qr[:, n, :], start=True, stop=True)
                zt_done = pe.done(m)
                yield
                if l < 5:
                    x_made = dve.done(on(dve, z_done).tensor_tensor(xr[:, :, :], xr[:, :, :], sys4(by), ALU.add))
                    yield
                q_made = dve.done(on(dve, zt_done).tensor_tensor(qr[:, :, :], qr[:, :, :], sys4(bz), ALU.add))
                yield
            wait(pe, q_made, nat_made)
            for n in range(4):
                a, i = divmod(n, 2)
                m = pe.engine.matmul(bx[:, n * RW_D:(n + 1) * RW_D], gr[:, n, 2, :], vb_n[:, i, a * RW_D:(a + 1) * RW_D], start=True, stop=True)
            nv_done = pe.done(m)
            yield
            for n in range(4):
                a, i = divmod(n, 2)
                c = slice(RW_D * a, RW_D * (a + 1))
                m = pe.engine.matmul(by[c, i * P:(i + 1) * P], ka_n[:, 2 + i, c], qr[:, n, :], start=True, stop=True)
            xa_done = pe.done(m)
            yield
            nv_made = act.done(on(act, nv_done).activation(nv[:, :, :], bx[:, 0:4 * RW_D].rearrange("p (s c) -> p s c", s=4), ACT.Copy))
            yield
            for n in range(4):
                m = on(pe, nv_made).matmul(bz[:, n * RW_D:(n + 1) * RW_D], qr[:, n, :], nv[:, n, :], start=True, stop=True)
            uv_done = pe.done(m)
            yield
            act.done(on(act, xa_done).activation(xa_T[:, :], by[:, 0:T], ACT.Copy))
            yield
            u_made = act.done(on(act, uv_done).activation(ur[:, :, :], bz[:, 0:4 * RW_D].rearrange("p (s c) -> p s c", s=4), ACT.Copy))
            yield
            for chunk in range(4):
                i, r0 = chunk // 2, RW_C * (chunk % 2)
                rows = slice(r0, r0 + RW_C)
                if chunk:
                    m = on(pe, z_made, u_made).matmul(bx[rows, 0:P], xa_T[:, chunk * RW_C:(chunk + 1) * RW_C], zs[:, chunk, :],
                                                      start=True, stop=True)
                    u_made = dve.done(on(dve, pe.done(m)).tensor_tensor(u_of(rows, i), u_of(rows, i), heads2(bx[rows, 0:P]), ALU.add))
                    yield
                if chunk < 3:
                    on(pe, u_made).matmul(by[:, 0:P], ka_n[rows, i, :], vb_n[rows, i, :], start=True, stop=False)
                    m = pe.engine.matmul(by[:, 0:P], vb_n[rows, 2 + i, :], u_of(rows, i), start=False, stop=True)
                    dve.done(on(dve, pe.done(m)).tensor_tensor(zs[:, chunk + 1, :], zs[:, chunk, :], by[:, 0:P], ALU.add))
                    yield
                    z_made = dve.done(on(dve, exps).scalar_tensor_tensor(
                        out=zs[:, chunk + 1, :], in0=zs[:, chunk + 1, :], scalar=e_state[:, chunk:chunk + 1], in1=p.c("blockones"),
                        op0=ALU.mult, op1=ALU.mult))
                    yield
            wait(pe, u_made, z_made)
            for n in range(4):
                a, i = divmod(n, 2)
                c = slice(RW_D * a, RW_D * (a + 1))
                o_at = bz[:, n * RW_D:(n + 1) * RW_D]
                pe.engine.matmul(o_at, gr[:, n, 3, :], vb_n[:, i, c], start=True, stop=False, skip_group_check=True)
                m = pe.engine.matmul(o_at, gr[:, n, 1, :], ur[:, n, :], start=False, stop=True, skip_group_check=True)
            within = pe.done(m)
            yield
            for chunk in range(4):
                i, r0 = chunk // 2, RW_C * (chunk % 2)
                m = pe.engine.matmul(bx[r0:r0 + RW_C, i * P:(i + 1) * P], ar[:, i, 1, r0:r0 + RW_C], zs[:, chunk, :],
                                     start=True, stop=True)
            across = pe.done(m)
            yield
            d = act.done(on(act, within).activation(orw[:, :, :], bz[:, 0:4 * RW_D].rearrange("p (s c) -> p s c", s=4), ACT.Copy))
            yield
            o_at = orw[:, :, :].rearrange("p (a t) c -> p t a c", a=2)
            dve.done(on(dve, across, d).tensor_tensor(o_at, o_at, bx[:, 0:2 * P].rearrange("p (t a c) -> p t a c", t=2, a=2), ALU.add))
            yield
            dve.done(on(dve).tensor_reduce(stat[:, 1, :], orw[:, :, :], AX.X, ALU.add))
            yield
            dve.done(on(dve).tensor_scalar(stat[:, 1, :], stat[:, 1, :], 1.0 / RW_D, None, ALU.mult))
            yield
            d = dve.done(on(dve).tensor_tensor(orw[:, :, :], orw[:, :, :], bc(stat[:, 1, :].unsqueeze(2), P, 4, RW_D), ALU.subtract))
            yield
            a = act.done(on(act, d).activation(osq[:, :, :], orw[:, :, :], ACT.Square))
            yield
            dve.done(on(dve, a).tensor_reduce(stat[:, 2, :], osq[:, :, :], AX.X, ALU.add))
            yield
            d = dve.done(on(dve).tensor_scalar(stat[:, 2, :], stat[:, 2, :], 1.0 / RW_D, RW_EPS, ALU.mult, ALU.add))
            yield
            r = pool.done(on(pool, d).tensor_tensor(stat[:, 3, :], stat[:, 2, :], p.minus_half[:, 0:4], ALU.pow))
            yield
            by_tile = orw[:, :, :].rearrange("p (a t) c -> p t a c", a=2)
            d = dve.done(on(dve, r).tensor_tensor(osq[:, :, :].rearrange("p (t a) c -> p t a c", a=2), by_tile,
                                                  bc(stat[:, 3, :].rearrange("p (a t) -> p t a", a=2).unsqueeze(3), P, 2, 2, RW_D), ALU.mult))
            yield
            for i in range(NT):
                m = on(pe, d).transpose(by[:, i * P:(i + 1) * P], osq[:, 2 * i:2 * i + 2, :].rearrange("p a c -> p (a c)"), ident)
            dve.done(on(dve, pe.done(m)).tensor_scalar(sqr[:, :], by[:, 0:T], col(LN_W), col(LN_B), ALU.mult, ALU.add))
            yield
            dve.done(on(dve).tensor_tensor(sqr[:, :], sqr[:, :], bv[:, :], ALU.add))
            yield
            dve.done(on(dve, gT).tensor_tensor(rbuf[:, ds(q, 1), :].rearrange("p a t -> p (a t)"), sqr[:, :], gate_T[:, :], ALU.mult))
            yield

        def keep_kv(g, done):
            wait(act, kv_sem[g].now())
            return on(act, done).activation(kv_out[g][:, :], s.banks[g][:, :], ACT.Copy)

        def mix_turn(n, kind, pieces):
            turn_start[:] = [x.now() for x in p.lanes]
            p.join(act, dve, pool)
            interleave(p, gdn_head=gdn_head(n), rwkv_pair=rwkv_pair(n), **{kind: pieces})

        def kv_stores(store_of):
            for g in range(2):
                wait(act, (s.evacuated[g], s.block_no.at))
                p.dma(act, kv_sem[g], store_of(g), kv_out[g][:, :])

        wait(pe, mem_ready)
        with p.loop("mix_k", 4) as loop:
            mix_turn(loop.i, "k_block", s.block(columns(w["xattn_wk"], loop.i * COLS), operand, True, keep_kv))
            kv_stores(lambda g: k_store[ds(loop.i * 4 + 2 * g, 2), :, :].rearrange("a p t -> p a t"))
        with p.loop("mix_v", 4) as loop:
            mix_turn(loop.i + 4, "v_block", s.block(columns(w["xattn_wv"], loop.i * COLS), operand, False, keep_kv))
            kv_stores(lambda g: v_store[:, g, ds(loop.i * COLS, COLS)])
        x_free = s.last_used()
        split_T(mixg, 0, (dve.now(),), (x_free,))
        mixed = split_T(rbuf[:, 0:GDN_H, :], GDN_H, (dve.now(),), ())
        p.join()
        mix_ctx.close()
        h = p.sb("h", [P, NT, D])
        h_in = p.dma(act, load_x, h[:, :, :], x_tok)

        def add_to_h(first, scale=None):
            def read(g, done):
                wait(dve, h_in, (s.evacuated[g], s.block_no.at + (-1)))
                part = h[:, g, ds(first, COLS)]
                if scale is None:
                    return on(dve, done).tensor_tensor(part, part, s.banks[g][:, :], ALU.add)
                return on(dve, done).scalar_tensor_tensor(out=part, in0=part, scalar=scale, in1=s.banks[g][:, :],
                                                          op0=ALU.mult, op1=ALU.add)
            return read

        def h_done():
            return [(s.evacuated[g], s.block_no.at) for g in range(NT)]

        wait(pe, mixed)
        with p.loop("w_out", D // COLS) as loop:
            run(s.block(columns(w["w_out"], loop.i * COLS), operand, False, add_to_h(loop.i * COLS)))
        xa_ctx = ctx.enter_context(ExitStack())

        def xa_tile(name, *shape):
            return p.sb("xa_" + name, [P, *shape], ctx=xa_ctx)

        xk, xv, xo = xa_tile("k_T", KT, T), xa_tile("v", NT, D), xa_tile("o_T", KT, T)
        qh, vh = xa_tile("head_q_T", XD // P, T), xa_tile("head_v", NT, XD)
        e, e_T = xa_tile("weights", NT, T), xa_tile("weights_T", NT, T)
        mx, den = xa_tile("max", NT), xa_tile("sum", NT)
        load_kv = p.dma_sem("kv_arrived")
        p.join(act)
        wait(act, *[k.now() for k in kv_sem])
        p.dma(act, load_kv, xk[:, :, :], k_store.rearrange("k p t -> p k t"))
        kv_in = p.dma(act, load_kv, xv[:, :, :], v_store)
        q_ready = norm_to_operand(p, h, NORM_EPS, lambda ct: pcol("norm_xattn", ct), operand, after=h_done(),
                                  free=(s.last_used(),))

        def keep_q(g, done):
            return on(act, done).activation(qh[:, 2 * g:2 * g + 2, :].rearrange("p a b -> p (a b)"),
                                            s.banks[g][:, :], ACT.Copy)

        def cross_head(n):
            b0, b1, b2, b3 = p.ps[2:6]
            left = s.block_no.at
            tok = {}

            def scores():
                wait(pe, kv_in, *[(s.evacuated[g], left) for g in range(2)], *[x.now() for x in (act, dve)])
                for i in range(NT):
                    for c in range(XD // P):
                        m = pe.engine.matmul(b0[:, i * T:(i + 1) * T], qh[:, c, i * P:(i + 1) * P],
                                             xk[:, ds(n * (XD // P) + c, 1), :].rearrange("p a t -> p (a t)"),
                                             start=c == 0, stop=c == XD // P - 1)
                tok["s"] = pe.done(m)
                tok["v"] = dve.done(on(dve, kv_in, pe.now()).tensor_copy(vh[:, :, :], xv[:, :, ds(n * XD, XD)]))

            def maxima():
                s2 = b0[:, :].rearrange("p (t m) -> p t m", t=NT)
                dve.done(on(dve, tok["s"]).tensor_reduce(mx[:, :], s2, AX.X, ALU.max))
                tok["m"] = dve.done(on(dve).tensor_scalar(mx[:, :], mx[:, :], -XD ** -0.5, None, ALU.mult))
                for i in range(NT):
                    tok["e"] = act.done(on(act, tok["m"]).activation(
                        e[:, i, :], b0[:, i * T:(i + 1) * T], ACT.Exp, scale=XD ** -0.5, bias=mx[:, i:i + 1],
                        accum_out=den[:, i:i + 1]))

            def normalise():
                dve.done(on(dve, tok["e"]).reciprocal(den[:, :], den[:, :]))
                d = dve.done(on(dve).tensor_tensor(e[:, :, :], e[:, :, :], bc(den[:, :].unsqueeze(2), P, NT, T), ALU.mult))
                for i in range(NT):
                    for m_ in range(NT):
                        m = on(pe, d).transpose(b1[:, m_ * T + i * P:m_ * T + (i + 1) * P], e[:, i, m_ * P:(m_ + 1) * P], ident)
                tok["t"] = act.done(on(act, pe.done(m)).activation(e_T[:, :, :].rearrange("p a b -> p (a b)"), b1[:, :], ACT.Copy))

            def values():
                wait(pe, tok["t"], tok["v"])
                for c in range(XD // P):
                    for m_ in range(NT):
                        o = (b2, b3)[c // 2][:, (c % 2) * T:(c % 2 + 1) * T]
                        m = pe.engine.matmul(o, vh[:, m_, c * P:(c + 1) * P], e_T[:, m_, :], start=m_ == 0, stop=m_ == NT - 1)
                tok["o"] = pe.done(m)

            def outputs():
                for c in range(2):
                    act.done(on(act, tok["o"]).activation(
                        xo[:, ds(n * (XD // P) + 2 * c, 2), :].rearrange("p a b -> p (a b)"), (b2, b3)[c][:, :], ACT.Copy))
            return [scores, maxima, normalise, values, outputs]

        wait(pe, q_ready)
        wq = w["xattn_wq"]
        run(s.block(columns(wq, 0), operand, True, keep_q))
        with p.loop("cross_attention", XH - 1) as loop:
            steps = cross_head(loop.i)
            weave(s.block(columns(wq, (loop.i + 1) * COLS), operand, True, keep_q), steps, 32, first=1)
        for step in cross_head(XH - 1):
            step()
        wait(pe, split_T(xo[:, :, :], 0, (act.now(),), (s.last_used(),)))
        with p.loop("xattn_wo", D // COLS) as loop:
            run(s.block(columns(w["xattn_wo"], loop.i * COLS), operand, False, add_to_h(loop.i * COLS)))
        xa_ctx.close()
        mlp_ctx = ctx.enter_context(ExitStack())
        relu = [p.sb(f"mlp_relu{g}", [P, 2, T], ctx=mlp_ctx) for g in range(2)]
        hid = [p.sb("mlp_hidden_" + x, [P, KT, T], F32R, ctx=mlp_ctx) for x in ("head", "rest")]
        p.join()
        wait(pe, norm_to_operand(p, h, NORM_EPS, lambda ct: pcol("norm_mlp", ct), operand, after=h_done(),
                                 free=(s.last_used(),)))

        def keep_relu(g, done):
            return on(act, done, pool.now(), dve.now()).activation(relu[g][:, :, :].rearrange("p a b -> p (a b)"),
                                                                   s.banks[g][:, :], ACT.Relu)

        def square(first):
            def after(g):
                r, at = relu[g][:, :, :], ds(first + 2 * g, 2)
                d = pool.done(on(pool, (s.evacuated[g], s.block_no.at)).tensor_tensor(r, r, r, ALU.mult))
                a = act.done(on(act, d).activation(hid[0][:, at, :], r, ACT.Copy))
                dve.done(on(dve, a).tensor_tensor(hid[1][:, at, :], r, hid[0][:, at, :].bitcast(F32), ALU.subtract))
            return after

        with p.loop("mlp", D_FF // D) as quarter:
            with p.loop("mlp_up", D // COLS) as loop:
                run(s.block(columns(w["mlp_w_up"], quarter.i * D + loop.i * COLS), operand, True, keep_relu,
                            after=square(loop.i * (COLS // P))))
            hid_made, hid_early = dve.now(), (dve.sem, dve.at + (-NT))
            with p.loop("mlp_down", D // COLS) as loop:
                run(s.block(columns(w["mlp_w_down"], loop.i * COLS, rows=quarter.i * D), hid, False,
                            add_to_h(loop.i * COLS), ready=(hid_early,), late=(hid_made,)))
        mlp_ctx.close()
        p.join()
        fin_ctx = ctx.enter_context(ExitStack())
        fin_gain = p.sb("norm_final_rows", [P, D], ctx=fin_ctx)
        load_r = p.dma_sem("gain_rows_arrived")
        gain_in = p.dma(act, load_r, fin_gain[:, :], t["norm_final"].partition_broadcast(P))
        scaled = norm_scale(p, h_done(), h, NORM_EPS)
        for i in range(NT):
            normed = dve.done(on(dve, scaled, gain_in, act.now()).scalar_tensor_tensor(
                out=h[:, i, :], in0=h[:, i, :], scalar=p.rstd[:, i:i + 1], in1=fin_gain[:, :], op0=ALU.mult, op1=ALU.mult))
        x2_ready = to_operand(p, h, lambda i: ident, None, operand, after=(normed,), free=(s.last_used(),))
        fin_ctx.close()

        att_ctx = ctx.enter_context(ExitStack())

        def att_tile(name, *shape):
            return p.sb("att_" + name, [P, *shape], ctx=att_ctx)

        half_w = AH * AD
        halves_ = [dict(qk=att_tile(f"qk_T_{n}", 16, T), v=att_tile(f"v_{n}", NT, half_w), g=att_tile(f"gate_T_{n}", 8, T))
                   for n in "ab"]
        g_tanh = att_tile("gate_tanh", 2, T)
        bias_sems = [p.dma_sem(f"pair_bias_arrived{k}") for k in range(2)]
        stats2 = [[att_tile(f"{name}{k}", 2, NT) for name in ("max", "sum")] for k in range(2)]
        wide = lambda x: x.rearrange("p (a i) t -> p a i t", a=2)
        k_a, g_a = halves_[0]["qk"][:, 8:16, :], halves_[0]["g"]
        SETS = [(att_tile("pair_q_T", T), att_tile("pair_k_T", T), att_tile("pair_v", NT, P), att_tile("scores", 2, NT, T),
                 att_tile("weights_T", 2, NT, T), *stats2[0], [p.ps[k] for k in (2, 3, 2, 3, 4)], bias_sems[0]),
                (g_a[:, 0, :], g_a[:, 1, :], g_a[:, 2, :].rearrange("p (i c) -> p i c", i=NT), wide(k_a[:, 0:4, :]),
                 wide(k_a[:, 4:8, :]), *stats2[1], [p.ps[k] for k in (5, 6, 5, 6, 7)], bias_sems[1])]
        p.join()

        def keep_qk(half, first):
            def read(g, done):
                return on(act, done).activation(half["qk"][:, ds(first + 2 * g, 2), :].rearrange("p a b -> p (a b)"),
                                                s.banks[g][:, :], ACT.Copy)
            return read

        def keep_v(half, first):
            def read(g, done):
                return on(act, done).activation(half["v"][:, g, ds(first, COLS)], s.banks[g][:, :], ACT.Copy)
            return read

        def keep_g(half, first):
            def read(g, done):
                x = s.banks[g][:, :].rearrange("p (a t) -> p a t", a=2)
                free = (s.evacuated[1 - g], s.block_no.at + (g - 1))
                a = act.done(on(act, done, free).activation(g_tanh[:, :, :], x, ACT.Tanh, scale=0.5))
                return on(dve, a).scalar_tensor_tensor(out=half["g"][:, ds(first + 2 * g, 2), :], in0=g_tanh[:, :, :],
                                                       scalar=1.0, in1=x, op0=ALU.add, op1=ALU.mult)
            return read

        def t5_bias(n, a, i):
            base = bass.AP(t5_store.tensor, (NT - i) * P - 1, ap=[[P * 2 * T, AH], [2 * T - 1, P], [1, T]])
            return [(slice(0, P), base[ds(2 * n + a, 1), :, :].rearrange("h p j -> (h p) j"))]

        def na_bias(n, a, i):
            parts = []
            for r in range(2):
                at = GRID - 1 + (3 - 2 * i - r) * P
                base = bass.AP(na_store.tensor, at, ap=[[GRID * NA_ROW, AH], [NA_ROW - 1, GRID], [P, 4], [1, GRID]])
                parts.append((slice(GRID * r, GRID * (r + 1)), base[ds(2 * n + a, 1), :, :, :].rearrange("h p r j -> (h p) r j")))
            return parts

        def pair_attention(half, n, bias_of, masked, tiles=SETS[0]):
            qs2, ks2, vs2, sc, sc_T, a_max, a_sum, b, bias_sem = tiles
            tok = {}
            tile = lambda x, k: x[:, ds(k, 1), :].rearrange("p a t -> p (a t)")

            def stage():
                wait(act, dve.now(), pe.now())
                for a in range(2):
                    for i in range(NT):
                        for rows, src in bias_of(n, a, i):
                            dst = sc[rows, a, i, :]
                            if masked:
                                dst = dst.rearrange("p (r j) -> p r j", r=4)
                            tok["b"] = p.dma(act, bias_sem, dst, src)
                dve.done(on(dve, pe.now(), act.now()).tensor_copy(qs2[:, :], tile(half["qk"], n)))
                tok["qk"] = dve.done(on(dve).tensor_copy(ks2[:, :], tile(half["qk"], n + 8)))
                tok["v"] = dve.done(on(dve).tensor_copy(vs2[:, :, :], half["v"][:, :, ds(n * P, P)]))

            def scores():
                wait(pe, tok["qk"])
                for a in range(2):
                    c = slice(AD * a, AD * (a + 1))
                    for i in range(NT):
                        m = pe.engine.matmul(b[a][:, i * T:(i + 1) * T], qs2[c, i * P:(i + 1) * P], ks2[c, :], start=True, stop=True)
                    tok["s", a] = pe.done(m)

            def weigh(a):
                def step():
                    x = sc[:, a, :, :]
                    dve.done(on(dve, tok["s", a], tok["b"]).tensor_tensor(x, x, b[a][:, :].rearrange("p (t j) -> p t j", t=NT), ALU.add))
                    if masked:
                        x4 = sc[:, a, :, :].rearrange("p t (r j) -> p (t r) j", j=GRID)
                        dve.done(on(dve).tensor_tensor(x4, x4, bc(p.c("na_mask").unsqueeze(1), P, 4 * NT, GRID), ALU.add))
                    dve.done(on(dve).tensor_reduce(a_max[:, a, :], x, AX.X, ALU.max))
                    tok["m", a] = dve.done(on(dve).tensor_scalar(a_max[:, a, :], a_max[:, a, :], -AD ** -0.5, None, ALU.mult))
                return step

            def exps(a):
                def step():
                    for i in range(NT):
                        tok["e", a] = act.done(on(act, tok["m", a]).activation(sc[:, a, i, :], sc[:, a, i, :], ACT.Exp, scale=AD ** -0.5,
                                                                     bias=a_max[:, a, i:i + 1], accum_out=a_sum[:, a, i:i + 1]))
                return step

            def normalise(a):
                def step():
                    dve.done(on(dve, tok["e", a]).reciprocal(a_sum[:, a, :], a_sum[:, a, :]))
                    x = sc[:, a, :, :]
                    tok["w", a] = dve.done(on(dve).tensor_tensor(x, x, bc(a_sum[:, a, :].unsqueeze(2), P, NT, T), ALU.mult))
                return step

            def turn(a):
                def step():
                    wait(pe, tok["w", a])
                    for i in range(NT):
                        for k in range(NT):
                            m = pe.engine.transpose(b[2 + a][:, k * T + i * P:k * T + (i + 1) * P], sc[:, a, i, k * P:(k + 1) * P], ident)
                    tok["u", a] = pe.done(m)
                return step

            def keep(a):
                def step():
                    tok["t", a] = act.done(on(act, tok["u", a]).activation(sc_T[:, a, :, :].rearrange("p k t -> p (k t)"), b[2 + a][:, :], ACT.Copy))
                return step

            def values():
                wait(pe, tok["v"], tok["t", 1])
                for a in range(2):
                    c = slice(AD * a, AD * (a + 1))
                    for k in range(NT):
                        m = pe.engine.matmul(b[4][c, 0:T], vs2[:, k, c], sc_T[:, a, k, :], start=k == 0, stop=k == NT - 1)
                dve.done(on(dve, pe.done(m)).scalar_tensor_tensor(
                    out=tile(half["qk"], n), in0=b[4][:, 0:T], scalar=0.5, in1=tile(half["g"], n), op0=ALU.mult, op1=ALU.mult))

            return [stage, scores, weigh(0), exps(0), weigh(1), exps(1), normalise(0), turn(0), normalise(1), keep(0),
                    turn(1), keep(1), values]

        w2 = w["w_in_2"]
        wait(pe, x2_ready)
        KINDS = (("qk", 4, True, keep_qk, COLS // P), ("v", 2, False, keep_v, COLS), ("g", 2, True, keep_g, COLS // P))

        def projections(half, first, name, steps_of=None):
            at = 0
            for kind, n, transposed, keep, step in KINDS:
                with p.loop(name + kind, n) as loop:
                    block = s.block(columns(w2, (loop.i + at) * COLS + first), operand, transposed, keep(half, loop.i * step))
                    if steps_of:
                        weave(block, steps_of(loop.i + at), 32 if transposed else 16, first=1)
                    else:
                        run(block)
                at += n

        projections(halves_[0], 0, "a_")
        projections(halves_[1], 4 * half_w, "b_", lambda n: pair_attention(halves_[0], n, t5_bias, False))
        def pairs(first, tiles, behind=0):
            for _ in range(behind):
                yield
            for n in range(2):
                for step in pair_attention(halves_[1], first + n, na_bias, True, tiles):
                    step()
                    yield

        p.join()
        ya_ready = split_T(halves_[0]["qk"][:, 0:8, :], 0, (dve.now(),), (s.last_used(),))
        with p.loop("neighbourhood", 2) as loop:
            c = loop.i * (2 * COLS)
            p.join(act, dve)
            interleave(p, pairs_0=pairs(loop.i * 4, SETS[0]), pairs_1=pairs(loop.i * 4 + 2, SETS[1], behind=4),
                       w_out_block=s.block(half_columns(w["w_out_2"], c, 0), operand, False,
                                           (add_to_h(c, ALPHA), add_to_h(c + COLS, ALPHA)), ready=(ya_ready,), parts=2))

        y_ready = split_T(halves_[1]["qk"][:, 0:8, :], 8, (dve.now(),), (s.last_used(),))
        p.join()
        att_ctx.close()
        ln_rows = p.sb("ln_rows", [P, 2, D])
        normed = p.sb("ln_normed", [P, NT, D])
        ln_sums, ln_mean = p.sb("ln_sums", [P, NT, D // COLS]), p.sb("ln_mean", [P, NT])
        p.dma(act, load_r, ln_rows[:, 0, :], t["ln_gain_2"][0].partition_broadcast(P))
        ln_in = p.dma(act, load_r, ln_rows[:, 1, :], t["ln_bias_2"][0].partition_broadcast(P))

        def add_block(block):
            def read(g, done):
                part = h[:, g, block * COLS:(block + 1) * COLS]
                wait(dve, (s.evacuated[g], s.block_no.at + (-1)))
                return on(dve, done).tensor_tensor(part, part, s.banks[g][:, :], ALU.add)
            return read

        for n in range(2):
            run(s.block(half_columns(w["w_out_2"], 2 * n * COLS, half_w), operand, False,
                        (add_block(2 * n), add_block(2 * n + 1)), ready=(y_ready,), parts=2, first_kt=8, last=n == 1))
            for i in range(NT):
                for k in (2 * n, 2 * n + 1):
                    summed = dve.done(on(dve, (s.evacuated[i], s.block_no.at)).tensor_reduce(
                        ln_sums[:, i, k:k + 1], h[:, i, k * COLS:(k + 1) * COLS], AX.X, ALU.add))
        stored = p.dma_sem("out_stored")
        out_tok = out[0].rearrange("(t p) d -> p t d", p=P)
        dve.done(on(dve).tensor_reduce(ln_mean[:, :], ln_sums[:, :, :], AX.X, ALU.add))
        m = dve.done(on(dve).tensor_scalar(ln_mean[:, :], ln_mean[:, :], -1.0 / D, None, ALU.mult))
        for i in range(NT):
            sq = act.done(on(act, m, pe.now()).activation(p.junk[:, :], h[:, i, :], ACT.Square, bias=ln_mean[:, i:i + 1],
                                                          accum_out=p.ss[:, i:i + 1]))
            pool.done(on(pool, sq).tensor_scalar(p.ss[:, 2 + i:3 + i], p.ss[:, i:i + 1], 1.0 / D, LN_EPS, ALU.mult, ALU.add))
            r = pool.done(on(pool).tensor_tensor(p.rstd[:, i:i + 1], p.ss[:, 2 + i:3 + i], p.minus_half[:, 0:1], ALU.pow))
            for n in range(D // COLS):
                c = slice(n * COLS, (n + 1) * COLS)
                x = normed[:, i, c]
                dve.done(on(dve, r).tensor_scalar(x, h[:, i, c], ln_mean[:, i:i + 1], p.rstd[:, i:i + 1], ALU.add, ALU.mult))
                d = dve.done(on(dve, ln_in).tensor_tensor(x, x, ln_rows[:, 0, c], ALU.mult))
                adder = pool if n < 2 else dve
                wait(sp, adder.done(on(adder, d, ln_in).tensor_tensor(x, x, ln_rows[:, 1, c], ALU.add)))
                p.dma(sp, stored, out_tok[:, i, c], x)
        wait(sp, stored.now())
    return p


def kernel(**inputs):
    import concourse.bacc as bacc
    from concourse.bass_utils import run_bass_kernel_spmd

    arrays = {f"in_{name}_dram": np.ascontiguousarray(a) for name, a in dict(inputs, **constants()).items()}
    plan = {}
    for _ in range(2):
        nc = bacc.Bacc("TRN2", target_bir_lowering=False, num_devices=1)
        t = {name[3:-5]: nc.dram_tensor(name, a.shape, mybir.dt.from_np(a.dtype), kind="ExternalInput").ap()
             for name, a in arrays.items()}
        build_program(nc, t, nc.dram_tensor("out_0_dram", (1, T, D), F32, kind="ExternalOutput").ap(), plan)
    return run_bass_kernel_spmd(nc, [arrays], core_ids=[0]).results[0]["out_0_dram"]
```
